# Optimizing a Trainium2 kernel written in Bass

```python
import math
import jax
import jax.numpy as jnp
from jax import lax
import numpy as np

D_MODEL = 1024
BATCH = 1
SEQ = 1024
DEPTH = 1

RW_HEADS = 6
RW_HEAD_DIM = 64
RW_WIDTH = RW_HEADS * RW_HEAD_DIM
SB_HEADS = 6
SB_HEAD_DIM = 64
SB_WIDTH = SB_HEADS * SB_HEAD_DIM
POOL_WINDOWS = (2, 4, 8, 16)
POOL_GROUPS = 4
POOL_GROUP_DIM = 64
POOL_WIDTH = POOL_GROUPS * POOL_GROUP_DIM
MIX_WIDTH = RW_WIDTH + SB_WIDTH + POOL_WIDTH

RW_DECAY_RANK = 32
RW_ICLR_RANK = 32
RW_VRES_RANK = 32
RW_GATE_RANK = 64
RW_GN_EPS = 64e-5

RW_COLS = 3 * RW_WIDTH + RW_DECAY_RANK + RW_ICLR_RANK + RW_GATE_RANK
SB_COLS = 3 * SB_WIDTH
IN_COLS = RW_COLS + SB_COLS + POOL_WIDTH

SB_BLOCK = 128

N_EXPERTS = 64
TOP_K = 6
N_GROUPS = 8
TOPK_GROUPS = 4
EXPERT_DIM = 256
ROUTED_SCALE = 2.5
MOE_BLOCK = 128

RMS_EPS = 1e-6

kernel_name = "hybrid_rwkv7_stickbreak_pool_moe_adaln"

def rms_norm(x, eps=RMS_EPS):
    xf = x.astype(jnp.float32)
    return (xf * lax.rsqrt(jnp.mean(xf * xf, axis=-1, keepdims=True) + eps)).astype(x.dtype)

def token_shift(u, mu):
    prev = jnp.pad(u, ((0, 0), (1, 0), (0, 0)))[:, :-1]
    return u + (prev - u) * mu

def split_heads(t, n_heads, head_dim):
    return t.reshape(t.shape[0], t.shape[1], n_heads, head_dim)

def rwkv7_scan(r, w, k, v, a, b):
    B, S, H, N = r.shape
    xs = (jnp.moveaxis(r, 1, 0), jnp.moveaxis(w, 1, 0), jnp.moveaxis(k, 1, 0),
          jnp.moveaxis(v, 1, 0), jnp.moveaxis(a, 1, 0), jnp.moveaxis(b, 1, 0))

    def step(state, inp):
        r_t, w_t, k_t, v_t, a_t, b_t = inp
        sa = jnp.einsum('bhvk,bhk->bhv', state, a_t)
        state = (state * w_t[:, :, None, :] + sa[..., None] * b_t[:, :, None, :]
                 + v_t[..., None] * k_t[:, :, None, :])
        return state, jnp.einsum('bhvk,bhk->bhv', state, r_t)

    state0 = jnp.zeros((B, H, N, N), jnp.float32)
    _, ys = lax.scan(step, state0, xs)
    return jnp.moveaxis(ys, 0, 1)

def rwkv7_time_mix(p_rw, v_first, v_gate, w0, w2, a0, a2, g2, k_k, k_a, r_k, ln_g, ln_b):
    B, S, _ = p_rw.shape
    C = RW_WIDTH
    f = p_rw.astype(jnp.float32)
    r = f[..., :C]
    k = f[..., C:2 * C]
    v = f[..., 2 * C:3 * C]
    o = 3 * C
    xw = f[..., o:o + RW_DECAY_RANK]
    o += RW_DECAY_RANK
    xa = f[..., o:o + RW_ICLR_RANK]
    o += RW_ICLR_RANK
    xg = f[..., o:o + RW_GATE_RANK]

    w_log = -jax.nn.softplus(-(w0 + jnp.tanh(xw) @ w2)) - 0.5
    decay = jnp.exp(-jnp.exp(w_log))
    a = jax.nn.sigmoid(a0 + xa @ a2)
    if v_gate is not None:
        v = v + (v_first - v) * v_gate
    g = jax.nn.sigmoid(xg) @ g2

    kk = split_heads(k * k_k, RW_HEADS, RW_HEAD_DIM)
    kk = kk / jnp.maximum(jnp.sqrt(jnp.sum(kk * kk, axis=-1, keepdims=True)), 1e-12)
    k = k * (1.0 + (a - 1.0) * k_a)

    rh = split_heads(r, RW_HEADS, RW_HEAD_DIM)
    kh = split_heads(k, RW_HEADS, RW_HEAD_DIM)
    vh = split_heads(v, RW_HEADS, RW_HEAD_DIM)
    ah = split_heads(a, RW_HEADS, RW_HEAD_DIM)
    wh = split_heads(decay, RW_HEADS, RW_HEAD_DIM)
    y = rwkv7_scan(rh, wh, kh, vh, -kk, kk * ah)

    mean = jnp.mean(y, axis=-1, keepdims=True)
    var = jnp.mean(jnp.square(y - mean), axis=-1, keepdims=True)
    y = ((y - mean) * lax.rsqrt(var + RW_GN_EPS)).reshape(B, S, C) * ln_g + ln_b
    bonus = (jnp.sum(rh * kh * r_k, axis=-1, keepdims=True) * vh).reshape(B, S, C)
    return (y + bonus) * g, v

def stick_breaking_attention(q, k, v):
    S = q.shape[1]
    scale = SB_HEAD_DIM ** -0.5
    outs = []
    for i in range(S // SB_BLOCK):
        q0 = i * SB_BLOCK
        q1 = q0 + SB_BLOCK
        z = jnp.einsum('bqhd,bkhd->bhqk', q[:, q0:q1], k[:, :q1],
                       preferred_element_type=jnp.float32) * scale
        valid = jnp.arange(q0, q1)[:, None] > jnp.arange(q1)[None, :]
        log_not = jnp.where(valid, jax.nn.log_sigmoid(-z), 0.0)
        suffix = lax.cumsum(log_not, axis=3, reverse=True) - log_not
        att = jnp.where(valid, jnp.exp(jax.nn.log_sigmoid(z) + suffix), 0.0)
        outs.append(jnp.einsum('bhqk,bkhd->bqhd', att.astype(v.dtype), v[:, :q1]))
    return jnp.concatenate(outs, axis=1)

def multiscale_pool(u, w_pool, pool_scale):
    B, S, _ = u.shape
    ug = u.astype(jnp.float32).reshape(B, S, POOL_GROUPS, POOL_GROUP_DIM)
    positions = jnp.arange(1, S + 1, dtype=jnp.float32)
    pooled = []
    for g, win in enumerate(POOL_WINDOWS):
        xg = ug[:, :, g]
        cs = jnp.cumsum(xg, axis=1)
        cs_lag = jnp.pad(cs, ((0, 0), (win, 0), (0, 0)))[:, :S]
        count = jnp.minimum(positions, float(win))[None, :, None]
        pooled.append((cs - cs_lag) / count - xg)
    pooled = jnp.stack(pooled, axis=2)
    mixed = jnp.einsum('bsgc,gcd->bsgd', pooled, w_pool.astype(jnp.float32))
    return (mixed.reshape(B, S, POOL_WIDTH) * pool_scale).astype(u.dtype)

def swiglu(h, w_gate, w_up, w_down):
    return (jax.nn.silu(h @ w_gate) * (h @ w_up)) @ w_down

def routed_experts(hf, top_idx, top_w, w_gate, w_up, w_down):
    T, D = hf.shape
    n_assign = T * TOP_K
    n_blocks = -(-(n_assign + N_EXPERTS * MOE_BLOCK) // MOE_BLOCK)
    cap = n_blocks * MOE_BLOCK
    flat_e = top_idx.reshape(-1)
    flat_tok = jnp.repeat(jnp.arange(T, dtype=jnp.int32), TOP_K)
    flat_w = top_w.reshape(-1)
    order = jnp.argsort(flat_e)
    e_sorted = flat_e[order]
    counts = jnp.bincount(flat_e, length=N_EXPERTS)
    padded = (counts + MOE_BLOCK - 1) // MOE_BLOCK * MOE_BLOCK
    start = jnp.cumsum(counts) - counts
    pend = jnp.cumsum(padded)
    pstart = pend - padded
    dest = pstart[e_sorted] + (jnp.arange(n_assign) - start[e_sorted])
    slot_tok = jnp.full((cap,), T, jnp.int32).at[dest].set(flat_tok[order])
    slot_w = jnp.zeros((cap,), hf.dtype).at[dest].set(flat_w[order].astype(hf.dtype))
    block_e = jnp.minimum(
        jnp.searchsorted(pend, jnp.arange(n_blocks) * MOE_BLOCK, side='right'), N_EXPERTS - 1)
    h_pad = jnp.concatenate([hf, jnp.zeros((1, D), hf.dtype)], axis=0)

    def expert_block(args):
        tok, wts, e = args
        xb = h_pad[tok]
        yb = (jax.nn.silu(xb @ w_gate[e]) * (xb @ w_up[e])) @ w_down[e]
        return yb * wts[:, None]

    y = lax.map(expert_block, (slot_tok.reshape(n_blocks, MOE_BLOCK),
                               slot_w.reshape(n_blocks, MOE_BLOCK), block_e))
    return jax.ops.segment_sum(y.reshape(cap, D), slot_tok, num_segments=T + 1)[:T]

def moe_ffn(h, w_router, b_router, w_gate, w_up, w_down, ws_gate, ws_up, ws_down):
    B, S, D = h.shape
    T = B * S
    hf = h.reshape(T, D)
    scores = jax.nn.sigmoid(jnp.matmul(hf, w_router, preferred_element_type=jnp.float32))
    sel = scores + b_router.astype(jnp.float32)
    per_group = N_EXPERTS // N_GROUPS
    grp_score = jnp.sum(lax.top_k(sel.reshape(T, N_GROUPS, per_group), 2)[0], axis=-1)
    _, grp_idx = lax.top_k(grp_score, TOPK_GROUPS)
    grp_mask = jnp.any(grp_idx[..., None] == jnp.arange(N_GROUPS), axis=1)
    masked = jnp.where(jnp.repeat(grp_mask, per_group, axis=1), sel, -jnp.inf)
    _, top_idx = lax.top_k(masked, TOP_K)
    top_w = jnp.take_along_axis(scores, top_idx, axis=1)
    top_w = top_w / (jnp.sum(top_w, axis=-1, keepdims=True) + 1e-20) * ROUTED_SCALE
    routed = routed_experts(hf, top_idx, top_w, w_gate, w_up, w_down)
    shared = swiglu(hf, ws_gate, ws_up, ws_down)
    return (routed + shared).reshape(B, S, D)

def setup_inputs(seed: int = 0) -> dict:
    key = jax.random.key(seed)
    keys = iter(jax.random.split(key, 64))
    L = DEPTH
    Lv = DEPTH - 1
    D = D_MODEL

    def nrm(shape, scale):
        return jax.random.normal(next(keys), shape, jnp.float32) * scale

    def uni(shape, lo, hi):
        return jax.random.uniform(next(keys), shape, jnp.float32, lo, hi)

    return {
        "x": nrm((BATCH, SEQ, D), 1.0),
        "c": nrm((BATCH, D), 1.0),
        "w_ada": nrm((L, D, 6 * D), 0.5 * D ** -0.5),
        "b_ada": nrm((L, 6 * D), 0.02),
        "w_in": nrm((L, D, IN_COLS), D ** -0.5),
        "w_vres": nrm((Lv, D, RW_VRES_RANK), D ** -0.5),
        "mu_rw": uni((L, RW_COLS), 0.0, 1.0),
        "mu_vres": uni((Lv, RW_VRES_RANK), 0.0, 1.0),
        "rw_w0": uni((L, RW_WIDTH), -4.0, 1.0),
        "rw_w2": nrm((L, RW_DECAY_RANK, RW_WIDTH), 0.1 * RW_DECAY_RANK ** -0.5),
        "rw_a0": nrm((L, RW_WIDTH), 0.1),
        "rw_a2": nrm((L, RW_ICLR_RANK, RW_WIDTH), 0.5 * RW_ICLR_RANK ** -0.5),
        "rw_v0": nrm((Lv, RW_WIDTH), 0.5),
        "rw_v2": nrm((Lv, RW_VRES_RANK, RW_WIDTH), 0.5 * RW_VRES_RANK ** -0.5),
        "rw_g2": nrm((L, RW_GATE_RANK, RW_WIDTH), RW_GATE_RANK ** -0.5),
        "rw_k_k": 0.85 + nrm((L, RW_WIDTH), 0.05),
        "rw_k_a": 1.0 + nrm((L, RW_WIDTH), 0.05),
        "rw_r_k": nrm((L, RW_HEADS, RW_HEAD_DIM), 0.1),
        "rw_ln_g": 1.0 + nrm((L, RW_WIDTH), 0.05),
        "rw_ln_b": nrm((L, RW_WIDTH), 0.02),
        "sb_norm_g": 1.0 + nrm((L, SB_WIDTH), 0.05),
        "pool_w": nrm((L, POOL_GROUPS, POOL_GROUP_DIM, POOL_GROUP_DIM), POOL_GROUP_DIM ** -0.5),
        "pool_scale": uni((L, POOL_WIDTH), 0.5, 1.5),
        "w_out": nrm((L, MIX_WIDTH, D), MIX_WIDTH ** -0.5),
        "w_router": nrm((L, D, N_EXPERTS), D ** -0.5),
        "b_router": nrm((L, N_EXPERTS), 0.01),
        "w_exp_gate": nrm((L, N_EXPERTS, D, EXPERT_DIM), D ** -0.5),
        "w_exp_up": nrm((L, N_EXPERTS, D, EXPERT_DIM), D ** -0.5),
        "w_exp_down": nrm((L, N_EXPERTS, EXPERT_DIM, D), EXPERT_DIM ** -0.5),
        "w_sh_gate": nrm((L, D, EXPERT_DIM), D ** -0.5),
        "w_sh_up": nrm((L, D, EXPERT_DIM), D ** -0.5),
        "w_sh_down": nrm((L, EXPERT_DIM, D), EXPERT_DIM ** -0.5),
        "g_final": 1.0 + nrm((D,), 0.05),
    }

def reference(x, c, w_ada, b_ada, w_in, w_vres, mu_rw, mu_vres, rw_w0, rw_w2, rw_a0, rw_a2,
              rw_v0, rw_v2, rw_g2, rw_k_k, rw_k_a, rw_r_k, rw_ln_g, rw_ln_b, sb_norm_g,
              pool_w, pool_scale, w_out, w_router, b_router, w_exp_gate, w_exp_up, w_exp_down,
              w_sh_gate, w_sh_up, w_sh_down, g_final):
    B, S, D = x.shape
    cond = jax.nn.silu(c)
    v_first = None
    for l in range(DEPTH):
        mod = cond @ w_ada[l] + b_ada[l]
        sh_m, sc_m, gt_m, sh_f, sc_f, gt_f = (m[:, None, :] for m in jnp.split(mod, 6, axis=-1))

        h = rms_norm(x) * (1.0 + sc_m) + sh_m
        w_in_l = w_in[l] if l == 0 else jnp.concatenate([w_in[l], w_vres[l - 1]], axis=1)
        proj = h @ w_in_l
        p_rw = token_shift(proj[..., :RW_COLS], mu_rw[l])
        p_sb = proj[..., RW_COLS:RW_COLS + SB_COLS]
        p_pool = proj[..., RW_COLS + SB_COLS:IN_COLS]

        if l == 0:
            v_gate = None
        else:
            p_vres = token_shift(proj[..., IN_COLS:], mu_vres[l - 1]).astype(jnp.float32)
            v_gate = jax.nn.sigmoid(rw_v0[l - 1] + p_vres @ rw_v2[l - 1])
        rw_out, v_l = rwkv7_time_mix(p_rw, v_first, v_gate, rw_w0[l], rw_w2[l], rw_a0[l],
                                     rw_a2[l], rw_g2[l], rw_k_k[l], rw_k_a[l], rw_r_k[l],
                                     rw_ln_g[l], rw_ln_b[l])
        if l == 0:
            v_first = v_l

        q_sb = split_heads(p_sb[..., :SB_WIDTH], SB_HEADS, SB_HEAD_DIM)
        k_sb = split_heads(p_sb[..., SB_WIDTH:2 * SB_WIDTH], SB_HEADS, SB_HEAD_DIM)
        v_sb = split_heads(p_sb[..., 2 * SB_WIDTH:], SB_HEADS, SB_HEAD_DIM)
        sb_out = stick_breaking_attention(q_sb, k_sb, v_sb)
        sb_out = (rms_norm(sb_out) * sb_norm_g[l].reshape(SB_HEADS, SB_HEAD_DIM)).reshape(B, S, SB_WIDTH)

        pool_out = multiscale_pool(p_pool, pool_w[l], pool_scale[l])

        mixed = jnp.concatenate([rw_out.astype(x.dtype), sb_out.astype(x.dtype), pool_out], axis=-1)
        x = x + gt_m * (mixed @ w_out[l])

        h = rms_norm(x) * (1.0 + sc_f) + sh_f
        ffn = moe_ffn(h, w_router[l], b_router[l], w_exp_gate[l], w_exp_up[l], w_exp_down[l],
                      w_sh_gate[l], w_sh_up[l], w_sh_down[l])
        x = x + gt_f * ffn.astype(x.dtype)

    return rms_norm(x) * g_final


_drawn_inputs = setup_inputs


def setup_inputs(seed=0):
    import zlib

    import numpy as np

    out = dict(_drawn_inputs(seed))
    spreads = {}
    factors = {'rw_w2': 6.175,
     'rw_a0': 3.307,
     'rw_k_k': 3.742,
     'rw_k_a': 3.086,
     'rw_ln_g': 3.324,
     'rw_ln_b': 4.602}
    for name, (base, spread) in spreads.items():
        noise = np.random.default_rng([zlib.crc32(name.encode()), seed]).standard_normal(out[name].shape)
        drawn = base * np.exp(spread * noise) if base else spread * noise
        out[name] = jnp.asarray(drawn.astype(out[name].dtype))
    for name, factor in factors.items():
        out[name] = (out[name] * factor).astype(out[name].dtype)
    return out
```

```python
from contextlib import ExitStack

import concourse.bass as bass
from concourse import mybir

F32 = mybir.dt.float32
I32 = mybir.dt.int32
U32 = mybir.dt.uint32
ALU = mybir.AluOpType
ACT = mybir.ActivationFunctionType
AX = mybir.AxisListType

P = 128
NEG_BIG = -1.0e30


class Steps:

    body = None

    def __init__(self, known, key, sem):
        self.known, self.key, self.sem = known, key, sem
        self.n, self.labels = 0, {}

    def total(self):
        return self.known.get(self.key, {}).get("", 1)

    def step(self, name=None):
        self.n += 1
        if name is not None:
            assert name not in self.labels, name
            self.labels[name] = self.n

    def value(self, n, index=None, back=0):
        index = Steps.body if index is None else index
        if index is None:
            return n
        return (index + (1 - back)) * self.total() + n

    def at(self, name, index=None, back=0):
        return self.value(self.known.get(self.key, {}).get(name, 1), index, back)

    def last_of(self, names):
        return self.value(max(self.known.get(self.key, {}).get(n, 1) for n in names))

    def here(self):
        return self.value(self.n)

    def close(self):
        if self.n == 0:
            self.n = 1
        self.known[self.key] = dict(self.labels, **{"": self.n})


def build(nc, ins, out, known, stop=None, dump=None):
    f = {k: v for k, v in ins.items()}
    T = f["x"].shape[1]
    D = f["x"].shape[2]
    DK = D // P
    TT = T // P
    HALF = 512
    NH = T // HALF
    C = 64
    RW = f["rw_w0"].shape[1]
    SB = f["sb_norm_g"].shape[1]
    PW = f["pool_scale"].shape[1]
    PAIRS = RW // P
    RWC = f["mu_rw"].shape[1]
    LOWR = 3 * RW
    QC, KC, VC = RWC, RWC + SB, RWC + 2 * SB
    POOLC = RWC + 3 * SB
    NE = f["w_router"].shape[2]
    TOPK, NG, TOPG = 6, 8, 4
    EG = NE // NG
    FD = f["w_exp_gate"].shape[3]
    FK = FD // P
    NB = (T * TOPK + NE * P) // P
    RSCALE = 2.5
    WBUF = 4
    EPS = 1e-6
    GN_EPS = 64e-5

    top = ExitStack()

    def sem(name):
        return top.enter_context(nc.semaphore(name))

    def at_ctx(ctx, name, shape, dt=F32):
        return ctx.enter_context(nc.sbuf_tensor(name, shape, dt))

    def phase(name):
        return [Steps(known, f"{name}.{e}", sem(f"{name}_{e}")) for e in
                ("tensor_done", "vector_done", "scalar_done", "pool_done")]

    bank = [top.enter_context(nc.psum_tensor(f"bank{i}", [P, 512], F32)) for i in range(8)]

    hpad = nc.dram_tensor("h_rows", [T + P, D], F32).ap()
    x1d = nc.dram_tensor("x1_rows", [T, D], F32).ap()
    xTd = nc.dram_tensor("x_transposed", [P, DK * T], F32).ap()
    accd = nc.dram_tensor("ffn_rows", [T + P, D], F32).ap()

    ident = at_ctx(top, "ident", [P, P])
    ones = at_ctx(top, "ones", [P, P])
    headsum = at_ctx(top, "headsum", [P, P])
    gt = at_ctx(top, "gt", [P, P])
    ge = at_ctx(top, "ge", [P, P])
    lt = at_ctx(top, "lt", [P, P])
    near_gt = at_ctx(top, "near_gt", [P, P])
    near_lt = at_ctx(top, "near_lt", [P, P])
    far_lt = at_ctx(top, "far_lt", [P, P])
    mod = at_ctx(top, "mod", [P, 6, DK])
    eps_rms = at_ctx(top, "eps_rms", [P, 1])
    eps_gn = at_ctx(top, "eps_gn", [P, 1])
    slots = at_ctx(top, "slots", [P, NB + 8, 2], I32)
    btab = at_ctx(top, "btab", [1, 4, NB + 8], I32)
    SH_M, SC_M, GT_M, SH_F, SC_F, GT_F = range(6)

    def done():
        for c in (top,):
            c.close()

    front = ExitStack()
    hT = at_ctx(front, "hT", [P, DK, T])
    mixed = at_ctx(front, "mixed", [P, 1 + DK, T])
    mixT = mixed[:, 1:1 + DK, :]

    early = ExitStack()
    cond = at_ctx(early, "cond", [P, DK])
    bada = at_ctx(early, "bada", [P, 6, DK])
    sbw = {n: at_ctx(early, f"sb_w{n}", [P, DK, P]) for n in "qkv"}
    wlate = [at_ctx(early, f"ada_late{b}", [P, 4, D]) for b in range(2)]
    alate = at_ctx(early, "ada_late_sum", [P, 4, D])
    sbw_in = {n: sem(f"sb_w{n}_in") for n in "qkv"}
    late_in = [sem(f"ada_late{b}_in") for b in range(2)]
    w_k = f["w_ada"][0].rearrange("(p k) n -> p k n", k=DK)

    def load_late(eng, k):
        eng.dma_start(wlate[k % 2][:].rearrange("p g n -> p (g n)"), w_k[:, k, 2 * D:6 * D]).then_inc(late_in[k % 2], 16)

    def load_sb(eng, pair):
        for n, c0 in zip("qkv", (QC, KC, VC)):
            eng.dma_start(sbw[n][:], f["w_in"][0].rearrange("(p k) n -> p k n", k=DK)
                          [:, :, bass.ds(pair * P + c0, P)]).then_inc(sbw_in[n], 16)

    def weight_rows(v, sums, rows, k, name):
        o_, r_ = (x[:].rearrange("p g n -> p (g n)") for x in (sums, rows))
        if k == 0:
            v(nc.vector.tensor_scalar(o_, r_, cond[:, 0:1], None, ALU.mult), name)
        else:
            v(nc.vector.scalar_tensor_tensor(out=o_, in0=r_, scalar=cond[:, k:k + 1], in1=o_, op0=ALU.mult,
                                             op1=ALU.add), name)

    def ada_products(sums, groups, out_, last=None):
        for g in range(groups):
            for j in range(DK):
                last = nc.tensor.matmul(out_[:, g * DK + j:g * DK + j + 1], sums[:, g, j::DK], ones[:, 0:1],
                                        start=True, stop=True, skip_group_check=True)
        return last

    with ExitStack() as s:
        xT = at_ctx(s, "xT", [P, DK, T])
        WA = 3
        wada = [at_ctx(s, f"wada{b}", [P, 2, D]) for b in range(WA)]
        asum = at_ctx(s, "ada_sum", [P, 2, D])
        cc = at_ctx(s, "cc", [P, DK])
        rstd = at_ctx(s, "rstd", [P, T])
        Tn, Vn, Sn, Pn = phase("front")
        ada_in = [sem(f"ada_in{b}") for b in range(WA)]
        x_in = [sem(f"x_in{i}") for i in range(TT)]
        c_in, b_in = sem("c_in"), sem("b_in")
        xT_saved = sem("xT_saved")
        xt = [mixT[:, i, :] for i in range(TT)]
        sq = [hT[:, k, :] for k in range(DK)]
        block = s.enter_context(nc.Block())

        @block.sync
        def _(sp):
            for i in range(TT):
                sp.dma_start(xt[i], f["x"][0][i * P:(i + 1) * P, :]).then_inc(x_in[i], 16)
            for k in range(DK):
                if k >= WA:
                    sp.wait_ge(Vn.sem, Vn.at(f"ada{k - WA}"))
                sp.dma_start(wada[k % WA][:].rearrange("p g n -> p (g n)"), w_k[:, k, 0:2 * D]).then_inc(ada_in[k % WA], 16)
            sp.wait_ge(Sn.sem, Sn.at(f"xT{TT - 1}"))
            sp.wait_ge(Vn.sem, Vn.at(f"xT{TT - 1}"))
            sp.dma_start(xTd, xT[:].rearrange("p k t -> p (k t)")).then_inc(xT_saved, 16)
            load_sb(sp, 0)
            load_late(sp, 0)
            load_late(sp, 1)
            sp.wait_ge(xT_saved, 16)

        @block.gpsimd
        def _(pool):
            pl = nc.gpsimd

            def p(ins, name=None):
                ins.then_inc(Pn.sem, 1)
                Pn.step(name)
                pool.wait_ge(Pn.sem, Pn.here())

            p(pl.memset(ones[:], 1.0))
            p(pl.affine_select(out=ident[:], in_=ones[:], compare_op=ALU.is_equal, fill=0.0, base=0,
                               pattern=[[-1, P]], channel_multiplier=1), "ident")
            p(pl.memset(eps_rms[:], EPS))
            p(pl.memset(eps_gn[:], GN_EPS))
            p(pl.affine_select(out=gt[:], in_=ones[:], compare_op=ALU.is_gt, fill=0.0, base=0,
                               pattern=[[1, P]], channel_multiplier=-1))
            p(pl.affine_select(out=ge[:], in_=ones[:], compare_op=ALU.is_ge, fill=0.0, base=0,
                               pattern=[[1, P]], channel_multiplier=-1))
            p(pl.affine_select(out=lt[:], in_=ones[:], compare_op=ALU.is_gt, fill=0.0, base=0,
                               pattern=[[-1, P]], channel_multiplier=1))

            def blocks(out, in_, n):
                v = [a[:].rearrange("p (b c) -> p b c", c=n) for a in (in_, out)]
                p(pl.affine_select(out=v[1], in_=v[0], compare_op=ALU.is_ge, fill=0.0, base=0,
                                   pattern=[[-n, P // n], [0, n]], channel_multiplier=1))
                p(pl.affine_select(out=v[1], in_=v[1], compare_op=ALU.is_ge, fill=0.0, base=n - 1,
                                   pattern=[[n, P // n], [0, n]], channel_multiplier=-1))

            blocks(headsum, ones, C)
            blocks(near_gt, gt, 16)
            blocks(near_lt, lt, 16)
            p(pl.tensor_tensor(far_lt[:], lt[:], near_lt[:], ALU.subtract), "masks")

        @block.scalar
        def _(act):
            def a(ins, name=None):
                ins.then_inc(Sn.sem, 1)
                Sn.step(name)

            act.dma_start(cc[:], f["c"].rearrange("b (p k) -> p (b k)", k=DK)).then_inc(c_in, 16)
            act.dma_start(bada[:], f["b_ada"][0].rearrange("(g p j) -> p g j", g=6, j=DK)).then_inc(b_in, 16)
            act.wait_ge(c_in, 16)
            a(nc.scalar.activation(cond[:], cc[:], ACT.Sigmoid), "csig")
            for i in range(TT):
                act.wait_ge(Tn.sem, Tn.at(f"x{i}b"))
                a(nc.scalar.activation(xT[:, 4:8, i * P:(i + 1) * P],
                                       bank[2 + i % 2][:].rearrange("p (k t) -> p k t", k=4), ACT.Copy), f"xT{i}")
            act.wait_ge(Sn.sem, Sn.here())
            act.wait_ge(Vn.sem, Vn.at(f"xT{TT - 1}"))
            for k in range(DK):
                a(nc.scalar.activation(sq[k], xT[:, k, :], ACT.Square), f"sq{k}")
            act.wait_ge(Pn.sem, Pn.at("masks"))
            for h in range(NH):
                act.wait_ge(Tn.sem, Tn.at(f"sum{h}"))
                a(nc.scalar.activation(rstd[:, h * HALF:(h + 1) * HALF], bank[5 + h][:], ACT.Sqrt,
                                       scale=1.0 / D, bias=eps_rms[:]), f"rms{h}")
            for k in range(DK):
                act.wait_ge(Vn.sem, Vn.at(f"scaled{k}"))
                a(nc.scalar.activation(hT[:, k, :], hT[:, k, :], ACT.Identity, bias=mod[:, SH_M, k:k + 1]))

        @block.tensor
        def _(pe):
            def t(ins, name=None):
                ins.then_inc(Tn.sem, 1)
                Tn.step(name)

            pe.wait_ge(Pn.sem, Pn.at("ident"))
            for i in range(TT):
                pe.wait_ge(x_in[i], 16)
                for half, n in ((0, "a"), (1, "b")):
                    if i >= 2:
                        R = Sn if half else Vn
                        pe.wait_ge(R.sem, R.at(f"xT{i - 2}"))
                    for q in range(4):
                        last = nc.tensor.transpose(bank[(2 if half else 0) + i % 2][:, q * P:(q + 1) * P],
                                                   xt[i][:, 4 * half + q::DK], ident[:])
                    t(last, f"x{i}{n}")
            for k in range(DK):
                pe.wait_ge(Sn.sem, Sn.at(f"sq{k}"))
                for h in range(NH):
                    last = nc.tensor.matmul(bank[5 + h][:], ones[:], sq[k][:, h * HALF:(h + 1) * HALF],
                                            start=(k == 0), stop=(k == DK - 1))
                    if k == DK - 1:
                        t(last, f"sum{h}")
            pe.wait_ge(Vn.sem, Vn.at(f"ada{DK - 1}"))
            t(ada_products(asum, 2, bank[4]), "ada")

        @block.vector
        def _(dve):
            def v(ins, name=None):
                ins.then_inc(Vn.sem, 1)
                Vn.step(name)

            dve.wait_ge(Sn.sem, Sn.at("csig"))
            v(nc.vector.tensor_tensor(cond[:], cond[:], cc[:], ALU.mult), "cond")
            for i in range(TT):
                dve.wait_ge(Tn.sem, Tn.at(f"x{i}a"))
                v(nc.vector.tensor_copy(xT[:, 0:4, i * P:(i + 1) * P],
                                        bank[i % 2][:].rearrange("p (k t) -> p k t", k=4)), f"xT{i}")

            def inv(h):
                c_ = slice(h * HALF, (h + 1) * HALF)
                dve.wait_ge(Sn.sem, Sn.at(f"rms{h}"))
                v(nc.vector.reciprocal(rstd[:, c_], rstd[:, c_]))

            for k in range(DK):
                dve.wait_ge(ada_in[k % WA], 16 * (k // WA + 1))
                dve.wait_ge(Vn.sem, Vn.here())
                weight_rows(v, asum, wada[k % WA], k, f"ada{k}")
                if k == DK - 3:
                    inv(0)
            inv(1)
            dve.wait_ge(b_in, 16)
            dve.wait_ge(Tn.sem, Tn.at("ada"))
            v(nc.vector.tensor_tensor(mod[:, SH_M:SC_M + 1, :].rearrange("p g j -> p (g j)"), bank[4][:, 0:2 * DK],
                                      bada[:, 0:2, :].rearrange("p g j -> p (g j)"), ALU.add))
            dve.wait_ge(Vn.sem, Vn.here())
            v(nc.vector.tensor_scalar(mod[:, SC_M, :], mod[:, SC_M, :], 1.0, None, ALU.add))
            dve.wait_ge(Vn.sem, Vn.here())
            for k in range(DK):
                v(nc.vector.scalar_tensor_tensor(out=hT[:, k, :], in0=xT[:, k, :], scalar=mod[:, SC_M, k:k + 1],
                                                 in1=rstd[:], op0=ALU.mult, op1=ALU.mult), f"scaled{k}")

        for x in (Tn, Vn, Sn, Pn):
            x.close()

    if stop == "front":
        return

    NSTEP = [(g, j) for g in range(NH) for j in reversed(range(4 * g + 4))]
    with ExitStack() as s:
        names = "qkv"
        w, w_in = sbw, sbw_in
        proj = {"q": 0, "k": 2, "v": 6}
        a_ = {n: at_ctx(s, f"sb_{n}", [P, T]) for n in names}
        vtok = at_ctx(s, "sb_vtok", [P, TT, P])
        zc = [at_ctx(s, f"sb_zc{b}", [P, HALF]) for b in range(2)]
        ez = [at_ctx(s, f"sb_ez{b}", [P, HALF]) for b in range(2)]
        spl = [at_ctx(s, f"sb_sp{b}", [P, HALF]) for b in range(4)]
        run = [at_ctx(s, f"sb_run{b}", [P, HALF]) for b in range(4)]
        att = [at_ctx(s, f"sb_att{b}", [P, HALF]) for b in range(4)]
        o = at_ctx(s, "sb_o", [P, T])
        osq = at_ctx(s, "sb_osq", [P, T])
        orn = at_ctx(s, "sb_orn", [P, T])
        negge = at_ctx(s, "sb_negle", [P, P])
        negone = at_ctx(s, "sb_negone", [P, P])
        gcols = at_ctx(s, "sb_gcols", [P, PAIRS + 1])
        gcur = at_ctx(s, "sb_gcur", [P, 1])
        Ta, Va, Sa, Pa = phase("attention")
        Tt, Vt, St, _ = phase("attention_tail")
        late_done = sem("ada_late_done")
        g_in = sem("sb_g_in")
        masks = sem("sb_masks")
        cap = at_ctx(s, "sb_cap", [P, P])
        steps = [(e, g, j) for e in range(2) for g, j in NSTEP]
        NS = len(steps)

        def cols(g, j):
            lo = max(j - 4 * g, 0) * P
            return lo, HALF, j >= 4 * g

        def zero_diag(dve, v, st):
            e, g, j = steps[st]
            lo, hi, diag = cols(g, j)
            if diag:
                dve.wait_ge(Sa.sem, Sa.at(f"att{st}"))
                v(nc.vector.tensor_tensor(att[st % 4][:, lo:lo + P], att[st % 4][:, lo:lo + P], cap[:], ALU.min),
                  f"zero{st}")

        def head_sums(t, pe, osq_done):
            for g in range(NH):
                pe.wait_ge(Sa.sem, osq_done(g))
                t(nc.tensor.matmul(bank[4 + g][:], headsum[:], osq[:, g * HALF:(g + 1) * HALF],
                                   start=True, stop=True), f"oss{g}")

        def head_rms(act, a, TS):
            for g in range(NH):
                act.wait_ge(TS.sem, TS.at(f"oss{g}"))
                a(nc.scalar.activation(orn[:, g * HALF:(g + 1) * HALF], bank[4 + g][:], ACT.Sqrt, scale=1.0 / C,
                                       bias=eps_rms[:]), f"rms{g}")

        def head_scale(dve, v, SS, VS, dest):
            for g in range(NH):
                c_ = slice(g * HALF, (g + 1) * HALF)
                dve.wait_ge(SS.sem, SS.at(f"rms{g}"))
                v(nc.vector.reciprocal(orn[:, c_], orn[:, c_]))
                dve.wait_ge(VS.sem, VS.here())
                v(nc.vector.scalar_tensor_tensor(out=o[:, c_], in0=o[:, c_], scalar=gcur[:], in1=orn[:, c_],
                                                 op0=ALU.mult, op1=ALU.mult))
                dve.wait_ge(VS.sem, VS.here())
                v(nc.vector.tensor_copy(dest(c_), o[:, c_]), f"mixed{g}")

        block = s.enter_context(nc.Block())

        @block.sync
        def _(sp):
            with nc.allow_non_contiguous_dma(reason="one gain per channel"):
                sp.dma_start(gcols[:, 1:PAIRS + 1], f["sb_norm_g"][0].rearrange("(t p) -> p t", p=P)).then_inc(g_in, 16)
            for k in range(2, DK):
                sp.wait_ge(late_done, k - 1)
                load_late(sp, k)
            with sp.Fori(0, PAIRS - 1) as i:
                sp.wait_ge(Ta.sem, Ta.at("v1", i))
                load_sb(sp, i + 1)

        @block.gpsimd
        def _(pool):
            pl = nc.gpsimd
            pool.wait_ge(masks, 7)
            pl.sem_inc(Ta.sem, Ta.total())
            pl.sem_inc(Va.sem, Va.total())
            pl.sem_inc(Sa.sem, Sa.total())
            pl.sem_inc(Pa.sem, Pa.total())
            with pool.Fori(0, PAIRS) as i:
                Steps.body = i

                def p(ins, name=None):
                    ins.then_inc(Pa.sem, 1)
                    Pa.step(name)

                for st, (e, g, j) in enumerate(steps):
                    lo, hi, diag = cols(g, j)
                    r, rn = run[st % 4], run[(st + 1) % 4]
                    pool.wait_ge(Va.sem, Va.at(f"sp{st}"))
                    if st >= 4:
                        pool.wait_ge(Ta.sem, Ta.at(f"acc{st - 3}"))
                    else:
                        pool.wait_ge(Ta.sem, Ta.at(f"pv{NS - 1}", i, 1))
                    pool.wait_ge(Pa.sem, Pa.here())
                    if diag:
                        p(pl.tensor_tensor(rn[:, lo:lo + P], spl[st % 4][:, lo:lo + P], ones[:], ALU.mult), None if lo + P < hi else f"run{st}")
                        if lo + P < hi:
                            p(pl.tensor_tensor(rn[:, lo + P:hi], r[:, lo + P:hi], spl[st % 4][:, lo + P:hi], ALU.add), f"run{st}")
                    else:
                        p(pl.tensor_tensor(rn[:], r[:], spl[st % 4][:], ALU.add), f"run{st}")

        @block.scalar
        def _(act):
            with act.Fori(0, PAIRS) as i:
                Steps.body = i

                def a(ins, name=None):
                    ins.then_inc(Sa.sem, 1)
                    Sa.step(name)

                for n in names:
                    if n == "v":
                        act.wait_ge(Va.sem, Va.at(f"mixed{NH - 1}", i, 1))
                        head_rms(act, a, Ta)
                    for h in range(NH):
                        act.wait_ge(Ta.sem, Ta.at(f"{n}{h}"))
                        act.wait_ge(Ta.sem, Ta.at(f"pv{NS - 1}", i, 1))
                        a(nc.scalar.activation(a_[n][:, h * HALF:(h + 1) * HALF], bank[proj[n] + h][:],
                                               ACT.Copy, scale=C ** -0.5 if n == "q" else 1.0), f"{n}{h}")
                nc.scalar.preload_act_table_set("natural_log_exp_and_others")
                for h in range(NH):
                    act.wait_ge(Ta.sem, Ta.at(f"vt{h}"))
                    a(nc.scalar.activation(vtok[:, 4 * h:4 * h + 4, :],
                                           bank[h][:].rearrange("p (k t) -> p k t", k=4), ACT.Copy), f"vt{h}")

                def weigh(st):
                    e, g, j = steps[st]
                    lo, hi, diag = cols(g, j)
                    act.wait_ge(Ta.sem, Ta.at(f"acc{st}"))
                    if st >= 4:
                        act.wait_ge(Ta.sem, Ta.at(f"pv{st - 4}"))
                    a(nc.scalar.activation(att[st % 4][:, lo:hi], bank[st % 4][:, lo:hi], ACT.Exp), f"att{st}")

                for st, (e, g, j) in enumerate(steps):
                    lo, hi, diag = cols(g, j)
                    act.wait_ge(Va.sem, Va.at(f"zc{st}"))
                    if st >= 2:
                        act.wait_ge(Va.sem, Va.at(f"sp{st - 2}"))
                    a(nc.scalar.activation(ez[st % 2][:, lo:hi], zc[st % 2][:, lo:hi], ACT.Exp))
                    act.wait_ge(Sa.sem, Sa.here())
                    a(nc.scalar.activation(ez[st % 2][:, lo:hi], ez[st % 2][:, lo:hi], ACT.Ln, bias=1.0), f"ln{st}")
                    if st >= 2:
                        weigh(st - 2)
                weigh(NS - 2)
                weigh(NS - 1)
                act.wait_ge(Ta.sem, Ta.at(f"pv{NS - 1}"))
                act.wait_ge(Va.sem, Va.at(f"mixed{NH - 1}"))
                for g in range(NH):
                    a(nc.scalar.activation(o[:, g * HALF:(g + 1) * HALF], bank[6 + g][:], ACT.Copy), f"o{g}")
                    act.wait_ge(Sa.sem, Sa.here())
                    a(nc.scalar.activation(osq[:, g * HALF:(g + 1) * HALF], o[:, g * HALF:(g + 1) * HALF],
                                           ACT.Square), f"osq{g}")
            Steps.body = None

            def at_(ins, name=None):
                ins.then_inc(St.sem, 1)
                St.step(name)

            act.wait_ge(Va.sem, Va.at(f"mixed{NH - 1}", PAIRS - 1))
            head_rms(act, at_, Tt)

        @block.vector
        def _(dve):
            nc.vector.memset(o[:], 0.0).then_inc(masks, 1)
            nc.vector.memset(osq[:], 0.0).then_inc(masks, 1)
            nc.vector.memset(gcols[:, 0:1], 0.0).then_inc(masks, 1)
            nc.vector.tensor_tensor(negge[:], lt[:], ident[:], ALU.add).then_inc(masks, 1)
            nc.vector.tensor_scalar(negone[:], ones[:], -1.0, None, ALU.mult).then_inc(masks, 1)
            nc.vector.tensor_scalar(cap[:], gt[:], 3.0e38, None, ALU.mult).then_inc(masks, 1)
            dve.wait_ge(masks, 6)
            nc.vector.tensor_scalar(negge[:], negge[:], -1.0, None, ALU.mult).then_inc(masks, 1)
            for k in range(DK):
                dve.wait_ge(late_in[k % 2], 16 * (k // 2 + 1))
                if k:
                    dve.wait_ge(late_done, k)
                weight_rows(lambda ins, name: ins.then_inc(late_done, 1), alate, wlate[k % 2], k, None)
            dve.wait_ge(g_in, 16)
            with dve.Fori(0, PAIRS) as i:
                Steps.body = i

                def v(ins, name=None):
                    ins.then_inc(Va.sem, 1)
                    Va.step(name)

                v(nc.vector.tensor_copy(gcur[:], gcols[:, bass.ds(i, 1)]), "gcur")
                head_scale(dve, v, Sa, Va,
                           lambda c_: mixed[:, bass.ds(i + PAIRS, 1), c_].rearrange("p a t -> p (a t)"))

                def soft(st):
                    e, g, j = steps[st]
                    lo, hi, diag = cols(g, j)
                    dve.wait_ge(Sa.sem, Sa.at(f"ln{st}"))
                    if st >= 4:
                        dve.wait_ge(Pa.sem, Pa.at(f"run{st - 4}"))
                        dve.wait_ge(Ta.sem, Ta.at(f"acc{st - 4}"))
                    v(nc.vector.tensor_tensor(spl[st % 4][:, lo:hi], bank[st % 4][:, lo:hi], ez[st % 2][:, lo:hi],
                                              ALU.max), None if diag else f"sp{st}")
                    if diag:
                        dve.wait_ge(Va.sem, Va.here())
                        v(nc.vector.tensor_tensor(spl[st % 4][:, lo:lo + P], spl[st % 4][:, lo:lo + P], gt[:],
                                                  ALU.mult), f"sp{st}")

                for st, (e, g, j) in enumerate(steps):
                    lo, hi, diag = cols(g, j)
                    dve.wait_ge(Ta.sem, Ta.at(f"z{st}"))
                    if st >= 2:
                        dve.wait_ge(Sa.sem, Sa.at(f"ln{st - 2}"))
                    v(nc.vector.tensor_scalar(zc[st % 2][:, lo:hi], bank[st % 4][:, lo:hi], 30.0, None, ALU.min),
                      f"zc{st}")
                    if st >= 1:
                        soft(st - 1)
                    if st >= 3:
                        zero_diag(dve, v, st - 3)
                soft(NS - 1)
                for st in (NS - 3, NS - 2, NS - 1):
                    zero_diag(dve, v, st)
            Steps.body = None

            def vt(ins, name=None):
                ins.then_inc(Vt.sem, 1)
                Vt.step(name)

            vt(nc.vector.tensor_copy(gcur[:], gcols[:, PAIRS:PAIRS + 1]))
            head_scale(dve, vt, St, Vt, lambda c_: mixT[:, 2 * PAIRS - 1, c_])
            dve.wait_ge(Tt.sem, Tt.at("ada"))
            vt(nc.vector.tensor_tensor(mod[:, GT_M:GT_F + 1, :].rearrange("p g j -> p (g j)"), bank[0][:, 0:4 * DK],
                                       bada[:, 2:6, :].rearrange("p g j -> p (g j)"), ALU.add))
            dve.wait_ge(Vt.sem, Vt.here())
            vt(nc.vector.tensor_scalar(mod[:, SC_F, :], mod[:, SC_F, :], 1.0, None, ALU.add))

        @block.tensor
        def _(pe):
            pe.wait_ge(masks, 7)
            with pe.Fori(0, PAIRS) as i:
                Steps.body = i

                def t(ins, name=None):
                    ins.then_inc(Ta.sem, 1)
                    Ta.step(name)

                for n in names:
                    pe.wait_ge(w_in[n], 16 * (i + 1))
                    if n == "v":
                        head_sums(t, pe, lambda g: Sa.at(f"osq{g}", i, 1))
                    for h in range(NH):
                        b = proj[n] + h
                        for k in range(DK):
                            last = nc.tensor.matmul(bank[b][:], w[n][:, k, :], hT[:, k, h * HALF:(h + 1) * HALF],
                                                    start=(k == 0), stop=(k == DK - 1))
                        t(last, f"{n}{h}")
                pe.wait_ge(Sa.sem, Sa.at("v1"))
                for h in range(NH):
                    for q in range(4):
                        last = nc.tensor.transpose(bank[h][:, q * P:(q + 1) * P],
                                                   a_["v"][:, (4 * h + q) * P:(4 * h + q + 1) * P], ident[:])
                    t(last, f"vt{h}")
                pe.wait_ge(Sa.sem, Sa.at("vt1"))
                for x in range(NS + 4):
                    if x < NS:
                        e, g, j = steps[x]
                        lo, hi, diag = cols(g, j)
                        hd = slice(C * e, C * e + C)
                        if x >= 4:
                            pe.wait_ge(Sa.sem, Sa.at(f"att{x - 4}"))
                        t(nc.tensor.matmul(bank[x % 4][:, lo:hi], a_["k"][hd, j * P:(j + 1) * P],
                                           a_["q"][hd, g * HALF + lo:g * HALF + hi], start=True, stop=True,
                                           skip_group_check=True), f"z{x}")
                    if 0 <= x - 2 < NS:
                        st = x - 2
                        e, g, j = steps[st]
                        lo, hi, diag = cols(g, j)
                        first = diag and lo + P == hi
                        pe.wait_ge(Va.sem, Va.at(f"sp{st}"))
                        last = nc.tensor.matmul(bank[st % 4][:, lo:hi], negge[:], spl[st % 4][:, lo:hi],
                                                start=False, stop=True, skip_group_check=True)
                        if not first:
                            l2 = lo + P if diag else lo
                            pe.wait_ge(Pa.sem, Pa.at(f"run{st - 1}"))
                            last = nc.tensor.matmul(bank[st % 4][:, l2:hi], negone[:], run[st % 4][:, l2:hi],
                                                    start=False, stop=True, skip_group_check=True)
                        t(last, f"acc{st}")
                    if x >= 4:
                        st = x - 4
                        e, g, j = steps[st]
                        lo, hi, diag = cols(g, j)
                        if diag:
                            pe.wait_ge(Va.sem, Va.at(f"zero{st}"))
                        pe.wait_ge(Sa.sem, Sa.at(f"att{st}"))
                        t(nc.tensor.matmul(bank[6 + g][C * e:C * e + C, lo:hi], vtok[:, j, C * e:C * e + C],
                                           att[st % 4][:, lo:hi], start=(j == 4 * g + 3), stop=True,
                                           skip_group_check=True), f"pv{st}")
            Steps.body = None

            def tt_(ins, name=None):
                ins.then_inc(Tt.sem, 1)
                Tt.step(name)

            head_sums(tt_, pe, lambda g: Sa.at(f"osq{g}", PAIRS - 1))
            pe.wait_ge(late_done, DK)
            tt_(ada_products(alate, 4, bank[0]), "ada")

        Steps.body = None
        for x in (Ta, Va, Sa, Pa, Tt, Vt, St):
            x.close()
    early.close()
    if stop == "attention":
        return

    low = ExitStack()
    lr = at_ctx(low, "lr", [P, T])
    R1 = f["rw_w2"].shape[1]
    R2 = R1 + f["rw_a2"].shape[1]
    with ExitStack() as s:
        tiles = ["p1", "p0", "lr"]
        w = {n: at_ctx(s, f"lp_w{n}", [P, DK, P]) for n in tiles}
        u = {n: at_ctx(s, f"lp_u{n}", [P, T + 16]) for n in tiles}
        Z = 16
        mu = at_ctx(s, "lp_mu", [P, 1])
        psc = at_ctx(s, "lp_psc", [P, 2])
        pw = [at_ctx(s, f"lp_pw{b}", [P, P]) for b in range(2)]
        dif = at_ctx(s, "lp_dif", [P, T])
        s2 = [at_ctx(s, f"lp_s{b}", [P, T + 16]) for b in range(2)]
        pos = at_ctx(s, "lp_pos", [P, T], I32)
        posf = at_ctx(s, "lp_posf", [P, T])
        rc = [at_ctx(s, f"lp_rc{b}", [P, T]) for b in range(2)]
        pd = [at_ctx(s, f"lp_pd{b}", [P, T]) for b in range(2)]
        Tl, Vl, Sl, Pl = phase("lowpool")
        w_in = {n: sem(f"lp_w{n}_in") for n in tiles}
        c_in = sem("lp_c_in")
        pw_in = sem("lp_pw_in")
        block = s.enter_context(nc.Block())

        @block.sync
        def _(sp):
            for n, c0 in zip(tiles, (POOLC + P, POOLC, LOWR)):
                sp.dma_start(w[n][:], f["w_in"][0].rearrange("(p k) n -> p k n", k=DK)[:, :, c0:c0 + P])\
                  .then_inc(w_in[n], 16)
            with nc.allow_non_contiguous_dma(reason="one value per channel"):
                sp.dma_start(mu[:], f["mu_rw"][0][LOWR:RWC].rearrange("(p a) -> p a", a=1)).then_inc(c_in, 16)
                sp.dma_start(psc[:], f["pool_scale"][0].rearrange("(t p) -> p t", p=P)).then_inc(c_in, 16)
            sp.wait_ge(Pl.sem, Pl.at("pwz"))
            for t in range(2):
                for g in range(2):
                    sp.dma_start(pw[t][g * C:(g + 1) * C, g * C:(g + 1) * C], f["pool_w"][0][2 * t + g]).then_inc(pw_in, 16)

        @block.gpsimd
        def _(pool):
            def p(ins, name=None):
                ins.then_inc(Pl.sem, 1)
                Pl.step(name)
            pl = nc.gpsimd
            for t in range(2):
                p(pl.memset(pw[t][:], 0.0), "pwz" if t else None)
            for n in tiles:
                p(pl.memset(u[n][:, 0:Z], 0.0))
            for b in range(2):
                p(pl.memset(s2[b][:, 0:Z], 0.0))
            p(pl.iota(pos[:], pattern=[[1, T]], base=1, channel_multiplier=0), "pos")

        @block.tensor
        def _(pe):
            def t_(ins, name=None):
                ins.then_inc(Tl.sem, 1)
                Tl.step(name)
            for x, n in enumerate(tiles):
                pe.wait_ge(w_in[n], 16)
                for h in range(NH):
                    for k in range(DK):
                        last = nc.tensor.matmul(bank[2 * x + h][:], w[n][:, k, :], hT[:, k, h * HALF:(h + 1) * HALF],
                                                start=(k == 0), stop=(k == DK - 1))
                    t_(last, f"{n}{h}")
            pe.wait_ge(pw_in, 16 * 4)
            for t in (1, 0):
                pe.wait_ge(Vl.sem, Vl.at(f"pd{t}"))
                for h in range(NH):
                    t_(nc.tensor.matmul(bank[2 * (1 - t) + h][:], pw[t][:], pd[t][:, h * HALF:(h + 1) * HALF],
                                        start=True, stop=True), f"mix{t}{h}")

        @block.scalar
        def _(act):
            def a(ins, name=None):
                ins.then_inc(Sl.sem, 1)
                Sl.step(name)
            for x, n in enumerate(tiles):
                if n == "lr":
                    act.wait_ge(c_in, 16 * 2)
                for h in range(NH):
                    act.wait_ge(Tl.sem, Tl.at(f"{n}{h}"))
                    a(nc.scalar.activation(u[n][:, Z + h * HALF:Z + (h + 1) * HALF], bank[2 * x + h][:], ACT.Copy), f"{n}{h}")
            for t in (1, 0):
                for h in range(NH):
                    act.wait_ge(Tl.sem, Tl.at(f"mix{t}{h}"))
                    a(nc.scalar.activation(mixT[:, 2 * PAIRS + t, h * HALF:(h + 1) * HALF], bank[2 * (1 - t) + h][:],
                                           ACT.Copy, scale=psc[:, t:t + 1]))
            act.wait_ge(Vl.sem, Vl.at("shifted"))
            a(nc.scalar.activation(lr[0:R1, :], dif[0:R1, :], ACT.Tanh))
            a(nc.scalar.activation(lr[R1:R2, :], dif[R1:R2, :], ACT.Copy))
            a(nc.scalar.activation(lr[R2:P, :], dif[R2:P, :], ACT.Sigmoid))

        @block.vector
        def _(dve):
            def v(ins, name=None):
                ins.then_inc(Vl.sem, 1)
                Vl.step(name)
                dve.wait_ge(Vl.sem, Vl.here())
            tt, ts = nc.vector.tensor_tensor, nc.vector.tensor_scalar
            dve.wait_ge(Pl.sem, Pl.at("pos"))
            v(nc.vector.tensor_copy(posf[:], pos[:]))
            WINS = ((2, 4), (8, 16))
            for t in (1, 0):
                for g, win in enumerate(WINS[t]):
                    hs = slice(g * C, (g + 1) * C)
                    v(ts(rc[t][hs, :], posf[hs, :], float(win), None, ALU.min))
                v(nc.vector.reciprocal(rc[t][:], rc[t][:]))
            for t in (1, 0):
                wins = WINS[t]
                dve.wait_ge(Sl.sem, Sl.at(f"p{t}1"))
                src, n, turn, have = u[f"p{t}"], 1, 0, {}
                while n < wins[1]:
                    dst = s2[turn]
                    if n * 2 > wins[0]:
                        v(tt(dst[C:P, Z:Z + T], src[C:P, Z:Z + T], src[C:P, Z - n:Z - n + T], ALU.add))
                        have[1] = dst
                    else:
                        v(tt(dst[:, Z:Z + T], src[:, Z:Z + T], src[:, Z - n:Z - n + T], ALU.add))
                        have[0] = dst
                    src, n, turn = dst, n * 2, 1 - turn
                for g in range(2):
                    hs = slice(g * C, (g + 1) * C)
                    v(tt(pd[t][hs, :], have[g][hs, Z:Z + T], rc[t][hs, :], ALU.mult))
                v(tt(pd[t][:], pd[t][:], u[f"p{t}"][:, Z:Z + T], ALU.subtract), f"pd{t}")
            dve.wait_ge(c_in, 16 * 2)
            dve.wait_ge(Sl.sem, Sl.at("lr1"))
            v(tt(dif[:], u["lr"][:, Z - 1:Z - 1 + T], u["lr"][:, Z:Z + T], ALU.subtract))
            v(nc.vector.scalar_tensor_tensor(out=dif[:], in0=dif[:], scalar=mu[:], in1=u["lr"][:, Z:Z + T],
                                             op0=ALU.mult, op1=ALU.add), "shifted")

        for x in (Tl, Vl, Sl, Pl):
            x.close()
    if stop == "lowpool":
        return

    CH = HALF // C
    Q = 4
    with ExitStack() as s:
        PRM = ["mu_r", "mu_k", "mu_v", "w0", "a0", "k_k", "k_a", "r_k", "ln_g", "ln_b"]
        prm = at_ctx(s, "rw_prm", [P, len(PRM), PAIRS])
        cur = at_ctx(s, "rw_cur", [P, len(PRM)])
        pc = {n: cur[:, x:x + 1] for x, n in enumerate(PRM)}
        w = {n: at_ctx(s, f"rw_w{n}", [P, DK, P]) for n in "rkv"}
        wl = at_ctx(s, "rw_wl", [P, P])
        u = {n: at_ctx(s, f"rw_u{n}", [P, 1 + HALF]) for n in "rkv"}
        E1 = {n: at_ctx(s, f"rw_{n}", [P, HALF]) for n in
              ("r", "k", "v0", "v1", "a", "g0", "g1", "kk", "logw", "eL", "enL", "reset", "y1")}
        E1.update(y2=mixT[:, PAIRS - 1, HALF:T], t1=mixT[:, PAIRS - 1, 0:HALF], L=mixed[:, 0, 0:HALF],
                  t2=mixed[:, 0, HALF:T])
        gate_ = [E1["g0"], E1["g1"]]
        value = [E1["v0"], E1["v1"]]
        last_ln = at_ctx(s, "rw_last_ln", [P, 2])
        bd = {n: at_ctx(s, f"rw_bd_{n}", [P, CH, P]) for n in ("a", "r", "b", "k", "v")}
        GB = {n: [at_ctx(s, f"rw_{n}{q}", [P, Q, P]) for q in range(2)] for n in
              ("Dt", "D", "N", "Aak", "Arb", "Ark", "At", "bt", "kt", "vt", "D2", "D2t", "R", "D4", "D4t")}
        S = [at_ctx(s, f"rw_S{b}", [P, P]) for b in range(2)]
        U = [at_ctx(s, f"rw_U{b}", [P, P]) for b in range(2)]
        Tr, Vr, Sr, Pr = phase("rwkv")
        Ty, Vy, Sy, Py = phase("rwkv_tail")
        w_in = {n: sem(f"rw_w{n}_in") for n in "rkv"}
        wl_in = sem("rw_wl_in")
        p_in = sem("rw_p_in")
        zeroed = sem("rw_zeroed")
        block = s.enter_context(nc.Block())

        @block.sync
        def _(sp):
            srcs = [f["mu_rw"][0][0:RW], f["mu_rw"][0][RW:2 * RW], f["mu_rw"][0][2 * RW:3 * RW], f["rw_w0"][0],
                    f["rw_a0"][0], f["rw_k_k"][0], f["rw_k_a"][0], f["rw_r_k"][0].rearrange("h d -> (h d)"),
                    f["rw_ln_g"][0], f["rw_ln_b"][0]]
            with nc.allow_non_contiguous_dma(reason="one value per channel"):
                for x, src in enumerate(srcs):
                    sp.dma_start(prm[:, x, :], src.rearrange("(t p) -> p t", p=P)).then_inc(p_in, 16)
            with sp.Fori(0, PAIRS) as i:
                Steps.body = i
                sp.wait_ge(Tr.sem, Tr.at("g_1", None, 1))
                for lo, hi, n in ((0, R1, "rw_w2"), (R1, R2, "rw_a2"), (R2, P, "rw_g2")):
                    sp.dma_start(wl[lo:hi, :], f[n][0][:, bass.ds(i * P, P)]).then_inc(wl_in, 16)
                for n in "krv":
                    x = "rkv".index(n)
                    sp.dma_start(w[n][:], f["w_in"][0].rearrange("(p k) n -> p k n", k=DK)
                                 [:, :, bass.ds(i * P + x * RW, P)]).then_inc(w_in[n], 16)
            Steps.body = None

        ZEROED = len(bd) + 10

        def chunked(ap):
            return ap.rearrange("p (c t) -> p c t", t=C)

        def halves(name):
            return [bd[name][e * C:(e + 1) * C, :, e * C:(e + 1) * C] for e in range(2)]

        def before(X, name, hf):
            return X.at(name.format(0)) if hf else X.at(name.format(1), None, 1)

        def head_mean(t, name):
            t(nc.tensor.matmul(bank[6][:], headsum[:], E1["y1"][:], start=True, stop=True), name)

        def head_var(t, name):
            t(nc.tensor.matmul(bank[7][:], headsum[:], E1["y1"][:], start=True, stop=True), name)

        def centre(v, name):
            v(nc.vector.scalar_tensor_tensor(out=E1["y2"][:], in0=bank[6][:], scalar=-1.0 / C, in1=E1["y1"][:],
                                             op0=ALU.mult, op1=ALU.add), name)

        def normalise(v, g_, b_, name):
            v(nc.vector.reciprocal(E1["y1"][:], E1["y1"][:]))
            v(nc.vector.tensor_tensor(E1["y2"][:], E1["y2"][:], E1["y1"][:], ALU.mult))
            v(nc.vector.tensor_scalar(E1["y2"][:], E1["y2"][:], g_, b_, ALU.mult, ALU.add), name)

        def finish_half(p, hf, dest, name):
            p(nc.gpsimd.tensor_tensor(E1["y2"][:], E1["y2"][:], value[hf][:], ALU.add))
            p(nc.gpsimd.tensor_tensor(dest, E1["y2"][:], gate_[hf][:], ALU.mult), name)

        @block.gpsimd
        def _(pool):
            pl = nc.gpsimd
            for n in bd:
                pl.memset(bd[n][:], 0.0).then_inc(zeroed, 1)
            for n in "rkv":
                pl.memset(u[n][:, 0:1], 0.0).then_inc(zeroed, 1)
            pl.memset(E1["reset"][:], 1.0).then_inc(zeroed, 1)
            for x in (E1["g1"], E1["v1"], E1["y1"], last_ln, cur):
                pl.memset(x[:], 0.0).then_inc(zeroed, 1)
            pool.wait_ge(zeroed, ZEROED - 1)
            pl.memset(E1["reset"][:].rearrange("p (c t) -> p c t", t=C)[:, :, 0:1], 0.0).then_inc(zeroed, 1)
            pool.wait_ge(zeroed, ZEROED)
            for X in (Tr, Vr, Sr, Pr):
                pl.sem_inc(X.sem, X.total())
            with pool.Fori(0, PAIRS) as i:
                Steps.body = i

                def p(ins, name=None):
                    ins.then_inc(Pr.sem, 1)
                    Pr.step(name)
                    pool.wait_ge(Pr.sem, Pr.here())
                e = {k: x[:] for k, x in E1.items()}
                ce = {k: chunked(x) for k, x in e.items()}
                for hf in range(NH):
                    ce["v"] = chunked(value[hf][:])
                    pool.wait_ge(Tr.sem, before(Tr, f"Y{{}}{CH - 1}", hf))
                    for name, op, src, ready in (("k", "k", "enL", ((Vr, "kf"), (Sr, "enL"))), ("r", "r", "eL", ((Vr, "r"),)),
                                                 ("v", "v", None, ((Vr, "v"),))):
                        for X, nm in ready:
                            pool.wait_ge(X.sem, X.at(f"{nm}{hf}"))
                        for x in range(2):
                            hs = slice(x * C, (x + 1) * C)
                            in1 = ce[src][hs] if src else ones[hs, 0:C].rearrange("p (a t) -> p a t", a=1).to_broadcast([C, CH, C])
                            p(pl.tensor_tensor(halves(name)[x], ce[op][hs], in1, ALU.mult), f"put_{name}{hf}" if x else None)
                    for q in range(2):
                        pool.wait_ge(Vr.sem, Vr.at(f"Dt{hf}{q}"))
                        p(pl.tensor_tensor(GB["R"][q][:], GB["Dt"][q][:],
                                           ident[:].rearrange("p (a t) -> p a t", a=1).to_broadcast([P, Q, P]), ALU.add),
                          f"R0{hf}{q}")
                    pool.wait_ge(Tr.sem, Tr.at(f"Arb{hf}1"))
                    for x in ("b", "k"):
                        for h in range(2):
                            hs = slice(h * C, (h + 1) * C)
                            p(pl.tensor_tensor(halves(x)[h], halves(x)[h],
                                               ce["eL"][:, :, C - 1:C][hs].to_broadcast([C, CH, C]), ALU.mult),
                              f"scaled{hf}" if x == "k" and h else None)
                    pool.wait_ge(Vr.sem, Vr.at(f"ln{hf}"))
                    finish_half(p, 1 - hf, mixed[:, bass.ds(i + hf, 1), (1 - hf) * HALF:(2 - hf) * HALF]
                                .rearrange("p a t -> p (a t)"), f"mix{hf}")
            Steps.body = None

            def py(ins, name=None):
                ins.then_inc(Py.sem, 1)
                Py.step(name)
                pool.wait_ge(Py.sem, Py.here())
            pool.wait_ge(Vy.sem, Vy.at("ln"))
            finish_half(py, 1, mixT[:, PAIRS - 1, HALF:T], "mix")

        INV = [("Ark", "k", "r"), ("Dt", "b", "a"), ("D", "a", "b"), ("Aak", "a", "k"), ("Arb", "b", "r")]
        order = [n for n, _, _ in INV] + ["At", "vt", "D2", "D2t", "bt", "kt", "R1", "D4", "D4t", "R2", "D8", "T1", "T",
                                          "G", "Gt", "F", "Hs", "X", "W1", "Z"]
        ON_VECTOR = ("Dt", "D", "Aak", "Arb", "Ark", "R1", "R2", "T1", "Hs")

        @block.tensor
        def _(pe):
            pe.wait_ge(zeroed, ZEROED)
            with pe.Fori(0, PAIRS) as i:
                Steps.body = i

                def t(ins, name=None):
                    ins.then_inc(Tr.sem, 1)
                    Tr.step(name)

                for hf in range(NH):
                    hc = slice(hf * HALF, (hf + 1) * HALF)
                    pe.wait_ge(Vr.sem, before(Vr, f"S{{}}{CH - 1}", hf))

                    def project(n):
                        b = "rkv".index(n)
                        pe.wait_ge(w_in[n], 16 * (i + 1))
                        for k in range(DK):
                            last = nc.tensor.matmul(bank[b][:], w[n][:, k, :], hT[:, k, hc], start=(k == 0),
                                                    stop=(k == DK - 1))
                        t(last, f"{n}_{hf}")

                    def low_rank(n):
                        lo, hi, b = {"w": (0, R1, 3), "a": (R1, R2, 4), "g": (R2, P, 5)}[n]
                        t(nc.tensor.matmul(bank[b][:], wl[lo:hi, :], lr[lo:hi, hc], start=True, stop=True), f"{n}_{hf}")

                    pe.wait_ge(wl_in, 48 * (i + 1))
                    low_rank("w")
                    project("k")
                    pe.wait_ge(Sr.sem, before(Sr, "y{}", hf))
                    head_mean(t, f"mean{hf}")
                    low_rank("a")
                    project("r")
                    pe.wait_ge(Sr.sem, Sr.at(f"sqy{hf}"))
                    head_var(t, f"var{hf}")
                    pe.wait_ge(Sr.sem, Sr.at(f"sq{hf}"))
                    t(nc.tensor.matmul(bank[6][:], headsum[:], E1["t1"][:], start=True, stop=True), f"kn{hf}")
                    project("v")
                    low_rank("g")
                    pe.wait_ge(Vr.sem, Vr.at(f"rk{hf}"))
                    pe.wait_ge(Sr.sem, Sr.at(f"std{hf}"))
                    t(nc.tensor.matmul(bank[7][:], headsum[:], E1["t2"][:], start=True, stop=True), f"bo{hf}")
                    pe.wait_ge(Sr.sem, Sr.at(f"g{hf}"))
                    bn = [0]

                    def stage(name, f1, f2, need, tr=False, banks=None):
                        for q in range(2):
                            b = bn[0] % 6
                            waits = [(e, f"{nm}{hf}{q}") for e, nm in need]
                            if bn[0] >= 6:
                                waits.append(evac[bn[0] - 6])
                            for e in (Vr, Sr, Pr):
                                on_e = [nm for x, nm in waits if x is e]
                                if on_e:
                                    pe.wait_ge(e.sem, e.last_of(on_e))
                            for c in range(Q):
                                if tr:
                                    last = nc.tensor.transpose(bank[b][:, c * P:(c + 1) * P], f1(q, c), ident[:])
                                else:
                                    last = nc.tensor.matmul(bank[b][:, c * P:(c + 1) * P], f1(q, c), f2(q, c),
                                                            start=True, stop=True)
                            t(last, f"{name}{hf}{q}")
                            who = Vr if name in ON_VECTOR else Sr
                            evac.append((who, f"{name}{hf}{q}"))
                            bn[0] += 1

                    evac = []
                    B = lambda n: (lambda q, c: bd[n][:, Q * q + c, :])
                    g = lambda n: (lambda q, c: GB[n][q][:, c, :])
                    pe.wait_ge(Pr.sem, Pr.at(f"put_r{hf}"))
                    for n, x, y in INV:
                        if n == "Dt":
                            pe.wait_ge(Vr.sem, Vr.at(f"put_b{hf}"))
                        stage(n, B(x), B(y), [])
                    stage("At", B("a"), None, [], tr=True)
                    pe.wait_ge(Pr.sem, Pr.at(f"put_v{hf}"))
                    stage("vt", B("v"), None, [], tr=True)
                    VD, SD = Vr, Sr
                    stage("D2", g("Dt"), g("D"), [(Vr, "Dt"), (Vr, "D")])
                    stage("D2t", g("D"), g("Dt"), [])
                    pe.wait_ge(Pr.sem, Pr.at(f"scaled{hf}"))
                    for n, x in (("bt", "b"), ("kt", "k")):
                        stage(n, B(x), None, [], tr=True)
                    stage("R1", g("D2"), g("R"), [(Sr, "D2"), (Pr, "R0")])
                    stage("D4", g("D2t"), g("D2"), [(Sr, "D2t")])
                    stage("D4t", g("D2"), g("D2t"), [])
                    stage("R2", g("D4"), g("R"), [(Sr, "D4"), (Vr, "R1")])
                    stage("D8", g("D4t"), g("D4"), [(Sr, "D4t")])
                    stage("T1", g("D"), g("R"), [(Sr, "D8"), (Vr, "R2")])
                    stage("T", g("R"), None, [(Vr, "T1")], tr=True)
                    stage("G", g("N"), g("R"), [(Vr, "N")])
                    stage("Gt", g("R"), g("N"), [])
                    stage("F", g("D4t"), g("D4"), [(Sr, "G"), (Sr, "Gt")])
                    stage("Hs", g("Dt"), g("N"), [(Sr, "F"), (Vr, "H")])
                    stage("X", g("D2t"), g("N"), [(Sr, "T"), (Vr, "Hs")])
                    stage("W1", g("At"), g("D2"), [(Sr, "X"), (Sr, "At")])
                    stage("Z", g("Aak"), g("D2"), [(Vr, "Aak")])
                    pe.wait_ge(Sr.sem, Sr.last_of([f"{nm}{hf}{q}" for nm in ("bt", "kt", "vt", "X", "W1", "Z")
                                                   for q in range(2)]))
                    for c in range(CH):
                        q, cc_ = divmod(c, Q)
                        St = S[c % 2]
                        nc.tensor.matmul(bank[c % 2][:, 0:P], g("D4t")(q, cc_), g("vt")(q, cc_), start=True, stop=False)
                        if c == 0:
                            pe.wait_ge(Vr.sem, Vr.at("S0") if hf == 0 else Vr.at(f"S{hf - 1}{CH - 1}"))
                        else:
                            pe.wait_ge(Vr.sem, Vr.at(f"S{hf}{c - 1}"))
                        t(nc.tensor.matmul(bank[c % 2][:, 0:P], g("D4")(q, cc_), St[:], start=False, stop=True), f"U{hf}{c}")
                        nc.tensor.matmul(bank[2 + c % 2][:, 0:P], g("kt")(q, cc_), g("vt")(q, cc_), start=True, stop=False)
                        pe.wait_ge(Vr.sem, Vr.at(f"U{hf}{c}"))
                        t(nc.tensor.matmul(bank[2 + c % 2][:, 0:P], g("bt")(q, cc_), U[c % 2][:], start=False, stop=True), f"S{hf}{c}")
                        yb = bank[4 + q][:, cc_ * P:(cc_ + 1) * P]
                        nc.tensor.matmul(yb, St[:], bd["r"][:, c, :], start=True, stop=False)
                        nc.tensor.matmul(yb, U[c % 2][:], g("Arb")(q, cc_), start=False, stop=False)
                        t(nc.tensor.matmul(yb, g("vt")(q, cc_), g("Ark")(q, cc_), start=False, stop=True), f"Y{hf}{c}")
            Steps.body = None

            def ty(ins, name=None):
                ins.then_inc(Ty.sem, 1)
                Ty.step(name)
            pe.wait_ge(Sr.sem, Sr.at("y1", PAIRS - 1))
            head_mean(ty, "mean")
            pe.wait_ge(Sy.sem, Sy.at("sqy"))
            head_var(ty, "var")

        @block.scalar
        def _(act):
            act.wait_ge(zeroed, ZEROED)
            with act.Fori(0, PAIRS) as i:
                Steps.body = i

                def a(ins, name=None):
                    ins.then_inc(Sr.sem, 1)
                    Sr.step(name)
                A = nc.scalar.activation
                act.wait_ge(Vr.sem, Vr.at("cur"))
                for hf in range(NH):
                    def evacuate(n):
                        act.wait_ge(Tr.sem, Tr.at(f"{n}_{hf}"))
                        act.wait_ge(Vr.sem, before(Vr, "shift_" + n + "{}", hf))
                        a(A(u[n][:, 1:1 + HALF], bank["rkv".index(n)][:], ACT.Copy), f"u{n}{hf}")
                    act.wait_ge(Tr.sem, Tr.at(f"w_{hf}"))
                    a(A(E1["logw"][:], bank[3][:], ACT.Sigmoid, bias=pc["w0"]), f"sig{hf}")
                    evacuate("k")
                    act.wait_ge(Tr.sem, Tr.at(f"a_{hf}"))
                    a(A(E1["a"][:], bank[4][:], ACT.Sigmoid, bias=pc["a0"]), f"a{hf}")
                    act.wait_ge(Vr.sem, Vr.at(f"cen{hf}"))
                    a(A(E1["y1"][:], E1["y2"][:], ACT.Square), f"sqy{hf}")
                    act.wait_ge(Vr.sem, Vr.at(f"kk0{hf}"))
                    a(A(E1["t1"][:], E1["kk"][:], ACT.Square), f"sq{hf}")
                    evacuate("r")
                    act.wait_ge(Tr.sem, Tr.at(f"var{hf}"))
                    a(A(E1["y1"][:], bank[7][:], ACT.Sqrt, scale=1.0 / C, bias=eps_gn[:]), f"std{hf}")
                    act.wait_ge(Tr.sem, Tr.at(f"kn{hf}"))
                    a(A(E1["t1"][:], bank[6][:], ACT.Sqrt), f"norm{hf}")
                    act.wait_ge(Vr.sem, Vr.at(f"Lp{hf}"))
                    a(A(E1["enL"][:], E1["L"][:], ACT.Exp, scale=-1.0))
                    a(A(E1["eL"][:], E1["L"][:], ACT.Exp), f"enL{hf}")
                    a(A(E1["logw"][:], E1["logw"][:], ACT.Exp), f"eLp{hf}")
                    evacuate("v")
                    act.wait_ge(Tr.sem, Tr.at(f"g_{hf}"))
                    act.wait_ge(Pr.sem, Pr.at("mix0") if hf else Pr.at("mix1", None, 1))
                    a(A(gate_[hf][:], bank[5][:], ACT.Copy), f"g{hf}")

                    def ev(name, dst):
                        for q in range(2):
                            act.wait_ge(Tr.sem, Tr.at(f"{name}{hf}{q}"))
                            b = order.index(name) * 2 + q
                            a(A(GB[dst][q][:].rearrange("p c t -> p (c t)"), bank[b % 6][:], ACT.Copy), f"{name}{hf}{q}")
                    for n, d in (("At", "At"), ("vt", "vt"), ("D2", "D2"), ("D2t", "D2t"), ("bt", "bt"), ("kt", "kt"),
                                 ("D4", "D4"), ("D4t", "D4t"), ("D8", "D"), ("T", "D2t"), ("G", "D4t"), ("Gt", "D4"),
                                 ("F", "Dt"), ("X", "D2"), ("W1", "D4"), ("Z", "D4t")):
                        ev(n, d)
                    for q in range(2):
                        act.wait_ge(Tr.sem, Tr.at(f"Y{hf}{Q * q + Q - 1}"))
                        for e in range(2):
                            a(A(chunked(E1["y1"][e * C:(e + 1) * C, :])[:, Q * q:Q * q + Q, :],
                                bank[4 + q][e * C:(e + 1) * C, :].rearrange("p (c t) -> p c t", t=P)
                                [:, :, e * C:(e + 1) * C], ACT.Copy), f"y{hf}" if q and e else None)
            Steps.body = None

            def ay(ins, name=None):
                ins.then_inc(Sy.sem, 1)
                Sy.step(name)
            act.wait_ge(Vy.sem, Vy.at("cen"))
            ay(A(E1["y1"][:], E1["y2"][:], ACT.Square), "sqy")
            act.wait_ge(Ty.sem, Ty.at("var"))
            ay(A(E1["y1"][:], bank[7][:], ACT.Sqrt, scale=1.0 / C, bias=eps_gn[:]), "std")

        @block.vector
        def _(dve):
            dve.wait_ge(zeroed, ZEROED)
            dve.wait_ge(p_in, 16 * len(PRM))
            with dve.Fori(0, PAIRS) as i:
                Steps.body = i

                def v(ins, name=None):
                    ins.then_inc(Vr.sem, 1)
                    Vr.step(name)
                    dve.wait_ge(Vr.sem, Vr.here())
                tt, ts, stt = nc.vector.tensor_tensor, nc.vector.tensor_scalar, nc.vector.scalar_tensor_tensor
                e = {k: x[:] for k, x in E1.items()}
                dve.wait_ge(Sr.sem, Sr.at("a1", None, 1))
                dve.wait_ge(Tr.sem, Tr.at(f"Y1{CH - 1}", None, 1))
                v(nc.vector.tensor_copy(last_ln[:], cur[:, PRM.index("ln_g"):PRM.index("ln_b") + 1]))
                v(nc.vector.tensor_copy(cur[:], prm[:, :, bass.ds(i, 1)].rearrange("p n a -> p (n a)")), "cur")
                v(nc.vector.memset(S[0][:], 0.0), "S0")
                for hf in range(NH):
                    e["v"] = value[hf][:]

                    def shift(n):
                        un, up = u[n][:, 1:1 + HALF], u[n][:, 0:HALF]
                        dve.wait_ge(Sr.sem, Sr.at(f"u{n}{hf}"))
                        v(tt(e[n], up, un, ALU.subtract))
                        v(stt(out=e[n], in0=e[n], scalar=pc["mu_" + n], in1=un, op0=ALU.mult, op1=ALU.add), f"{n}{hf}")
                        v(nc.vector.memset(u[n][:, 0:1], 0.0) if hf else
                          nc.vector.tensor_copy(u[n][:, 0:1], u[n][:, HALF:HALF + 1]), f"shift_{n}{hf}")

                    def put(name, op):
                        for x in range(2):
                            hs = slice(x * C, (x + 1) * C)
                            v(op(halves(name)[x], hs), f"put_{name}{hf}" if x else None)
                    ce = {k: chunked(x) for k, x in e.items()}
                    dve.wait_ge(Sr.sem, Sr.at(f"sig{hf}"))
                    v(ts(e["logw"], e["logw"], -0.6065306597126334, None, ALU.mult))
                    v(nc.vector.tensor_tensor_scan(e["L"], e["reset"], e["logw"], 0.0, ALU.mult, ALU.add))
                    v(tt(e["logw"], e["L"], e["logw"], ALU.subtract), f"Lp{hf}")
                    dve.wait_ge(Tr.sem, Tr.at(f"mean{hf}"))
                    dve.wait_ge(Pr.sem, Pr.at("mix0") if hf else Pr.at("mix1", None, 1))
                    centre(v, f"cen{hf}")
                    shift("k")
                    v(ts(e["kk"], e["k"], pc["k_k"], None, ALU.mult), f"kk0{hf}")
                    dve.wait_ge(Sr.sem, Sr.at(f"a{hf}"))
                    v(ts(e["t2"], e["a"], pc["k_a"], pc["k_a"], ALU.mult, ALU.subtract))
                    v(stt(out=e["k"], in0=e["t2"], scalar=1.0, in1=e["k"], op0=ALU.add, op1=ALU.mult), f"kf{hf}")
                    shift("r")
                    v(stt(out=e["t2"], in0=e["r"], scalar=pc["r_k"], in1=e["k"], op0=ALU.mult, op1=ALU.mult), f"rk{hf}")
                    dve.wait_ge(Sr.sem, Sr.at(f"norm{hf}"))
                    v(ts(e["t1"], e["t1"], 1e-12, None, ALU.max))
                    v(nc.vector.reciprocal(e["t1"], e["t1"]))
                    v(tt(e["kk"], e["kk"], e["t1"], ALU.mult))
                    v(tt(e["a"], e["kk"], e["a"], ALU.mult))
                    dve.wait_ge(Sr.sem, Sr.at(f"eLp{hf}"))
                    put("a", lambda o, h: stt(out=o, in0=ce["kk"][h], scalar=-1.0, in1=ce["logw"][h], op0=ALU.mult, op1=ALU.mult))
                    put("b", lambda o, h: tt(o, ce["a"][h], ce["enL"][h], ALU.mult))
                    shift("v")

                    def mask(m):
                        return m[:].rearrange("p (a t) -> p a t", a=1).to_broadcast([P, Q, P])

                    def src(name, q):
                        dve.wait_ge(Tr.sem, Tr.at(f"{name}{hf}{q}"))
                        return bank[(order.index(name) * 2 + q) % 6][:].rearrange("p (c t) -> p c t", t=P)
                    for q in range(2):
                        v(tt(GB["Ark"][q][:], src("Ark", q), mask(ge), ALU.mult), f"Ark{hf}{q}")
                    for q in range(2):
                        v(tt(GB["Dt"][q][:], src("Dt", q), mask(near_gt), ALU.mult), f"Dt{hf}{q}")
                    for q in range(2):
                        v(tt(GB["N"][q][:], src("D", q), mask(far_lt), ALU.mult), f"N{hf}{q}")
                        v(tt(GB["D"][q][:], src("D", q), mask(near_lt), ALU.mult), f"D{hf}{q}")
                    for n, m in (("Aak", lt), ("Arb", ge)):
                        for q in range(2):
                            v(tt(GB[n][q][:], src(n, q), mask(m), ALU.mult), f"{n}{hf}{q}")
                    dve.wait_ge(Tr.sem, Tr.at(f"bo{hf}"))
                    dve.wait_ge(Pr.sem, Pr.at(f"put_v{hf}"))
                    v(tt(value[hf][:], bank[7][:], e["v"], ALU.mult), f"bon{hf}")
                    dve.wait_ge(Sr.sem, Sr.at(f"std{hf}"))
                    ln = [pc["ln_g"], pc["ln_b"]] if hf else [last_ln[:, 0:1], last_ln[:, 1:2]]
                    normalise(v, *ln, f"ln{hf}")
                    for n in ("R1", "R2", "T1"):
                        for q in range(2):
                            v(tt(GB["R"][q][:], src(n, q), GB["R"][q][:], ALU.add), f"{n}{hf}{q}")
                    for q in range(2):
                        dve.wait_ge(Sr.sem, Sr.at(f"Gt{hf}{q}"))
                        v(tt(GB["N"][q][:], GB["D4t"][q][:], mask(ident), ALU.add), f"H{hf}{q}")
                    for q in range(2):
                        v(tt(GB["N"][q][:], src("Hs", q), GB["N"][q][:], ALU.add), f"Hs{hf}{q}")
                    for c in range(CH):
                        dve.wait_ge(Tr.sem, Tr.at(f"U{hf}{c}"))
                        if c >= 2:
                            dve.wait_ge(Tr.sem, Tr.at(f"Y{hf}{c - 2}"))
                        v(nc.vector.tensor_copy(U[c % 2][:], bank[c % 2][:, 0:P]), f"U{hf}{c}")
                        dve.wait_ge(Tr.sem, Tr.at(f"S{hf}{c}"))
                        if c >= 1:
                            dve.wait_ge(Tr.sem, Tr.at(f"Y{hf}{c - 1}"))
                        v(stt(out=S[(c + 1) % 2][:], in0=S[c % 2][:], scalar=E1["eL"][:, c * C + C - 1:c * C + C],
                              in1=bank[2 + c % 2][:, 0:P], op0=ALU.mult, op1=ALU.add), f"S{hf}{c}")
            Steps.body = None

            def vy(ins, name=None):
                ins.then_inc(Vy.sem, 1)
                Vy.step(name)
                dve.wait_ge(Vy.sem, Vy.here())
            dve.wait_ge(Ty.sem, Ty.at("mean"))
            dve.wait_ge(Pr.sem, Pr.at("mix1", PAIRS - 1))
            centre(vy, "cen")
            dve.wait_ge(Sy.sem, Sy.at("std"))
            normalise(vy, pc["ln_g"], pc["ln_b"], "ln")

        for x in (Tr, Vr, Sr, Pr, Ty, Vy, Sy, Py):
            x.close()
    low.close()
    if stop == "rwkv":
        return

    mid = ExitStack()
    xT = at_ctx(mid, "op_xT", [P, DK, T])
    wr = at_ctx(mid, "wr", [P, DK, NE])
    wg = at_ctx(mid, "ws_g", [P, DK, FD])
    wu = at_ctx(mid, "ws_u", [P, DK, FD])
    wd = at_ctx(mid, "ws_d", [P, FK, D])
    brow = at_ctx(mid, "rt_b", [P, NE])
    rt_in = {n: sem(f"rt_{n}_in") for n in ("r", "g", "u", "d", "b")}
    with ExitStack() as s:
        wo = at_ctx(s, "wo", [P, DK, D])
        sq = [at_ctx(s, f"op_sq{b}", [P, T]) for b in range(2)]
        rstd = at_ctx(s, "op_rstd", [P, T])
        zrow = at_ctx(s, "op_zrow", [P, D])
        To, Vo, So, Po = phase("outproj")
        wo_in = [sem(f"wo_in{k}") for k in range(DK)]
        xT_in = sem("op_xT_in")
        zsaved = sem("op_zsaved")
        block = s.enter_context(nc.Block())

        @block.sync
        def _(sp):
            for k in range(DK):
                sp.dma_start(wo[:, k, :], f["w_out"][0][k * P:(k + 1) * P, :]).then_inc(wo_in[k], 16)
            sp.dma_start(xT[:].rearrange("p k t -> p (k t)"), xTd).then_inc(xT_in, 16)
            sp.wait_ge(Po.sem, Po.at("zrow"))
            for dst in (hpad, accd):
                sp.dma_start(dst[T:T + P, :], zrow[:]).then_inc(zsaved, 16)
            sp.dma_start(wr[:], f["w_router"][0].rearrange("(p k) n -> p k n", k=DK)).then_inc(rt_in["r"], 16)
            sp.dma_start(brow[:], f["b_router"][0:1, :].to_broadcast([P, NE])).then_inc(rt_in["b"], 16)
            sp.dma_start(wg[:], f["w_sh_gate"][0].rearrange("(p k) n -> p k n", k=DK)).then_inc(rt_in["g"], 16)
            sp.dma_start(wu[:], f["w_sh_up"][0].rearrange("(p k) n -> p k n", k=DK)).then_inc(rt_in["u"], 16)
            sp.dma_start(wd[:], f["w_sh_down"][0].rearrange("(f p) n -> p f n", p=P)).then_inc(rt_in["d"], 16)
            sp.wait_ge(zsaved, 32)

        @block.gpsimd
        def _(pool):
            nc.gpsimd.memset(zrow[:], 0.0).then_inc(Po.sem, 1)
            Po.step("zrow")

        def sums(pe, t, j):
            pe.wait_ge(So.sem, So.at(f"sq{j}"))
            for h in range(NH):
                last = nc.tensor.matmul(bank[5 + h][:], ones[:], sq[j % 2][:, h * HALF:(h + 1) * HALF],
                                        start=(j == 0), stop=(j == DK - 1))
            t(last, f"sum{j}")

        @block.tensor
        def _(pe):
            def t(ins, name=None):
                ins.then_inc(To.sem, 1)
                To.step(name)
            def product(n, k):
                j, h = divmod(n, 2)
                return nc.tensor.matmul(bank[n % 4][:], wo[:, k, j::DK], mixT[:, k, h * HALF:(h + 1) * HALF],
                                        start=(k == 0), stop=(k == DK - 1))

            for k in range(DK):
                pe.wait_ge(wo_in[k], 16)
                for n in range(4):
                    last = product(n, k)
                    if k == DK - 1:
                        t(last, f"o{n}")
            for n in range(4, 2 * DK):
                pe.wait_ge(Vo.sem, Vo.at(f"x1_{n - 4}"))
                for k in range(DK):
                    last = product(n, k)
                t(last, f"o{n}")
                if n % 2:
                    sums(pe, t, n // 2 - 2)
            sums(pe, t, DK - 2)
            sums(pe, t, DK - 1)

        @block.scalar
        def _(act):
            def a(ins, name=None):
                ins.then_inc(So.sem, 1)
                So.step(name)
            for j in range(DK):
                act.wait_ge(Vo.sem, Vo.at(f"x1_{2 * j + 1}"))
                if j >= 2:
                    act.wait_ge(To.sem, To.at(f"sum{j - 2}"))
                a(nc.scalar.activation(sq[j % 2][:], xT[:, j, :], ACT.Square), f"sq{j}")
            act.wait_ge(To.sem, To.at(f"sum{DK - 1}"))
            for h in range(NH):
                a(nc.scalar.activation(rstd[:, h * HALF:(h + 1) * HALF], bank[5 + h][:], ACT.Sqrt, scale=1.0 / D,
                                       bias=eps_rms[:]), f"rms{h}")
            for k in range(DK):
                act.wait_ge(Vo.sem, Vo.at(f"scaled{k}"))
                a(nc.scalar.activation(hT[:, k, :], hT[:, k, :], ACT.Identity, bias=mod[:, SH_F, k:k + 1]), f"h{k}")

        @block.vector
        def _(dve):
            def v(ins, name=None):
                ins.then_inc(Vo.sem, 1)
                Vo.step(name)
            dve.wait_ge(xT_in, 16)
            for n in range(2 * DK):
                j, h = divmod(n, 2)
                c_ = slice(h * HALF, (h + 1) * HALF)
                dve.wait_ge(To.sem, To.at(f"o{n}"))
                v(nc.vector.scalar_tensor_tensor(out=xT[:, j, c_], in0=bank[n % 4][:], scalar=mod[:, GT_M, j:j + 1],
                                                 in1=xT[:, j, c_], op0=ALU.mult, op1=ALU.add), f"x1_{n}")
            for h in range(NH):
                c_ = slice(h * HALF, (h + 1) * HALF)
                dve.wait_ge(So.sem, So.at(f"rms{h}"))
                v(nc.vector.reciprocal(rstd[:, c_], rstd[:, c_]))
            dve.wait_ge(Vo.sem, Vo.here())
            for k in range(DK):
                v(nc.vector.scalar_tensor_tensor(out=hT[:, k, :], in0=xT[:, k, :], scalar=mod[:, SC_F, k:k + 1],
                                                 in1=rstd[:], op0=ALU.mult, op1=ALU.mult), f"scaled{k}")

        for x in (To, Vo, So, Po):
            x.close()
    if stop == "outproj":
        return

    with ExitStack() as s:
        actT = at_ctx(s, "sh_actT", [P, FK, T])
        gsig = [at_ctx(s, f"sh_sig{b}", [P, HALF]) for b in range(2)]
        trows = [mixT[:, b, :] for b in range(4)]
        rows = [mixT[:, 4 + b, :] for b in range(2)]
        place1 = [mixT[:, 6 + b, :].rearrange("t (i p) -> t i p", p=P) for b in range(2)]
        block1 = [at_ctx(s, f"rt_block_onehot{b}", [P, TT, 2, NB]) for b in range(2)]
        scT = at_ctx(s, "rt_scores_T", [NE, T])
        sc = at_ctx(s, "rt_scores", [P, TT, NE])
        sel = at_ctx(s, "rt_sel", [P, TT, NE])
        g8 = at_ctx(s, "rt_g8", [P, TT, NG, 8])
        gs = at_ctx(s, "rt_gs", [P, TT, NG])
        top8 = at_ctx(s, "rt_top8", [P, TT, 8])
        idx8 = at_ctx(s, "rt_idx8", [P, TT, 8], U32)
        idxf = at_ctx(s, "rt_idxf", [P, TT, 8])
        gmask = at_ctx(s, "rt_gmask", [P, TT, NG])
        tmp = at_ctx(s, "rt_tmp", [P, TT, NE])
        tmp2 = at_ctx(s, "rt_tmp2", [P, TT, NE])
        io_i = at_ctx(s, "rt_iota_i", [P, NE], I32)
        io_f = at_ctx(s, "rt_iota", [P, NE])
        blk_i = at_ctx(s, "rt_blk_i", [P, 1], I32)
        blk_f = at_ctx(s, "rt_blk", [P, 1])
        oh = [at_ctx(s, f"rt_onehot{j}", [P, TT, NE]) for j in range(TOPK)]
        M = at_ctx(s, "rt_M", [P, TT, NE])
        Mrun = at_ctx(s, "rt_Mrun", [P, TT + 1, NE])
        pick = at_ctx(s, "rt_pick", [P, TOPK, TT])
        wsum = at_ctx(s, "rt_wsum", [P, TT])
        rank = at_ctx(s, "rt_rank", [P, TT, NE])
        cnt = at_ctx(s, "rt_cnt", [P, NE])
        nb_ = at_ctx(s, "rt_nb", [P, NE])
        pend = at_ctx(s, "rt_pend", [P, NE])
        pst = at_ctx(s, "rt_pstart", [P, NE])
        slot = at_ctx(s, "rt_slot", [P, TT])
        slot_i = at_ctx(s, "rt_slot_i", [P, 2, TT], I32)
        slot_f = at_ctx(s, "rt_slot_f", [P, 2, TT])
        tok_f = at_ctx(s, "rt_tok", [P, TT])
        io_p = at_ctx(s, "rt_iota_place", [P, P], I32)
        io_pf = at_ctx(s, "rt_iota_placef", [P, P])
        tok_i = at_ctx(s, "rt_tok_i", [P, TT], I32)
        pad_i = at_ctx(s, "rt_pad_i", [P, 1], I32)
        pad_f = at_ctx(s, "rt_pad", [P, 1])
        entry = [at_ctx(s, f"rt_entry{b}", [P, 2, TT]) for b in range(TOPK)]
        be = at_ctx(s, "rt_be", [P, 4])
        buf_i = at_ctx(s, "rt_buffer_i", [P, 1], I32)
        some = at_ctx(s, "rt_some", [P, NE])
        Tq, Vq, Sq, Pq = phase("route")
        w_in = rt_in
        saved = [sem(f"sh_saved{b}") for b in range(2)]
        tsaved = [sem(f"rt_saved{b}") for b in range(4)]
        block = s.enter_context(nc.Block())

        @block.sync
        def _(sp):
            for i in range(TT):
                for x, dst in enumerate((x1d, hpad)):
                    n = 2 * i + x
                    sp.wait_ge(Sq.sem, Sq.at(f"half{2 * n + 1}"))
                    sp.dma_start(dst[i * P:(i + 1) * P, :], trows[n % 4]).then_inc(tsaved[n % 4], 16)
            for i in range(TT):
                sp.wait_ge(Vq.sem, Vq.at(f"sh{i}"))
                sp.wait_ge(Sq.sem, Sq.at(f"sh{i}"))
                sp.dma_start(accd[i * P:(i + 1) * P, :], rows[i % 2]).then_inc(saved[i % 2], 16)
            for b in range(4):
                sp.wait_ge(tsaved[b], 16 * (2 * TT // 4))
            for b in range(2):
                sp.wait_ge(saved[b], 16 * (TT // 2))

        @block.gpsimd
        def _(pool):
            def p(ins, name=None):
                ins.then_inc(Pq.sem, 1)
                Pq.step(name)
                pool.wait_ge(Pq.sem, Pq.here())
            pl = nc.gpsimd
            p(pl.memset(slots[:], 0))
            p(pl.iota(slots[:, :, 0:1].rearrange("p b a -> p (b a)"), pattern=[[0, NB + 8]], base=T, channel_multiplier=1))
            p(pl.iota(io_i[:], pattern=[[1, NE]], base=0, channel_multiplier=0))
            p(pl.iota(blk_i[:], pattern=[[0, 1]], base=-1, channel_multiplier=1))
            p(pl.iota(io_p[:], pattern=[[1, P]], base=0, channel_multiplier=0))
            p(pl.iota(tok_i[:], pattern=[[P, TT]], base=-T, channel_multiplier=1))
            p(pl.iota(pad_i[:], pattern=[[0, 1]], base=T, channel_multiplier=1), "iotas")
            for j in range(TOPK):
                pool.wait_ge(Vq.sem, Vq.at(f"hot{j}"))
                if j >= 2:
                    pool.wait_ge(Tq.sem, Tq.at(f"slots{j - 2}"))
                for x in (1, 0):
                    src = block1[j % 2][:, :, 0, :]
                    p(pl.tensor_tensor(block1[j % 2][:, :, x, :], src,
                                       entry[j][:, x, :].rearrange("p (i a) -> p i a", a=1).to_broadcast([P, TT, NB]),
                                       ALU.mult), None if x else f"hot{j}")

        @block.tensor
        def _(pe):
            def t(ins, name=None):
                ins.then_inc(Tq.sem, 1)
                Tq.step(name)
            pe.wait_ge(w_in["r"], 16)
            for h in range(NH):
                for k in range(DK):
                    last = nc.tensor.matmul(bank[h][0:NE, :], wr[:, k, :], hT[:, k, h * HALF:(h + 1) * HALF],
                                            start=(k == 0), stop=(k == DK - 1))
                t(last, f"scores{h}")
            for i in range(TT):
                pe.wait_ge(Sq.sem, Sq.at(f"scores{i // 4}"))
                last = nc.tensor.transpose(bank[2][:, i * NE:(i + 1) * NE], scT[:, i * P:(i + 1) * P], ident[0:NE, 0:NE])
            t(last, "scores")
            for n in range(4 * TT):
                i, x, half = n // 4, n // 2 % 2, n % 2
                if n >= 4:
                    pe.wait_ge(Sq.sem, Sq.at(f"half{n - 4}"))
                for q in range(4):
                    last = nc.tensor.transpose(bank[4 + n % 4][:, q * P:(q + 1) * P],
                                               (hT if x else xT)[:, 4 * half + q, i * P:(i + 1) * P], ident[:])
                t(last, f"half{n}")

            def gate_up(n):
                fk, h, x = n // 4, n // 2 % 2, n % 2
                for k in range(DK):
                    last = nc.tensor.matmul(bank[n % 4][:], (wu if x else wg)[:, k, fk * P:(fk + 1) * P],
                                            hT[:, k, h * HALF:(h + 1) * HALF], start=(k == 0), stop=(k == DK - 1))
                t(last, f"gu{n}")
            pe.wait_ge(w_in["g"], 16)
            pe.wait_ge(w_in["u"], 16)
            pe.wait_ge(Sq.sem, Sq.at("scores"))
            gate_up(0)
            pe.wait_ge(Sq.sem, Sq.at(f"half{4 * TT - 1}"))
            pe.wait_ge(Vq.sem, Vq.at("Mrun"))
            nc.tensor.matmul(bank[4][:], gt[:], M[:].rearrange("p i e -> p (i e)"), start=True, stop=False)
            nc.tensor.matmul(bank[4][:], ones[:], Mrun[:, 0:TT, :].rearrange("p i e -> p (i e)"), start=False, stop=True)
            t(nc.tensor.matmul(bank[5][:, 0:NE], ones[:], Mrun[:, TT, :], start=True, stop=True), "ranks")
            for n in range(1, 4):
                gate_up(n)
            for n in range(4, 8):
                pe.wait_ge(Vq.sem, Vq.at(f"act{(n - 4) // 2}"))
                gate_up(n)
            for j in range(TOPK):
                pe.wait_ge(Pq.sem, Pq.at(f"hot{j}"))
                for i in range(TT):
                    last = nc.tensor.matmul(bank[6][:, 0:2 * NB], place1[j % 2][:, i, :],
                                            block1[j % 2][:, i, :, :].rearrange("p x b -> p (x b)"),
                                            start=(j == 0 and i == 0), stop=(j == TOPK - 1 and i == TT - 1))
                t(last, f"slots{j}")
            pe.wait_ge(Vq.sem, Vq.at("blocks"))
            for x in range(4):
                last = nc.tensor.matmul(bank[7][0:1, x * P:(x + 1) * P], be[:, x:x + 1], ident[:], start=True, stop=True,
                                        skip_group_check=True)
            t(last, "table")
            pe.wait_ge(w_in["d"], 16)
            pe.wait_ge(Vq.sem, Vq.at(f"act{2 * FK - 1}"))
            for i in range(TT):
                for h in range(2):
                    if i >= 2:
                        R = Sq if h else Vq
                        pe.wait_ge(R.sem, R.at(f"sh{i - 2}"))
                    for fk in range(FK):
                        last = nc.tensor.matmul(bank[2 * (i % 2) + h][:], actT[:, fk, i * P:(i + 1) * P],
                                                wd[:, fk, h * HALF:(h + 1) * HALF], start=(fk == 0), stop=(fk == FK - 1))
                    t(last, f"down{i}{h}")

        @block.scalar
        def _(act):
            def a(ins, name=None):
                ins.then_inc(Sq.sem, 1)
                Sq.step(name)
            for h in range(NH):
                act.wait_ge(Tq.sem, Tq.at(f"scores{h}"))
                a(nc.scalar.activation(scT[:, h * HALF:(h + 1) * HALF], bank[h][0:NE, :], ACT.Sigmoid), f"scores{h}")
            act.wait_ge(Tq.sem, Tq.at("scores"))
            a(nc.scalar.activation(sc[:].rearrange("p i e -> p (i e)"), bank[2][:], ACT.Copy), "scores")
            for n in range(4 * TT):
                half = n % 2
                b = n // 2 % 4
                act.wait_ge(Tq.sem, Tq.at(f"half{n}"))
                if n >= 8:
                    act.wait_ge(tsaved[b], 16 * (n // 8))
                a(nc.scalar.activation(trows[b].rearrange("t (p j) -> t j p", j=DK)[:, 4 * half:4 * half + 4, :],
                                       bank[4 + n % 4][:].rearrange("t (j p) -> t j p", j=4), ACT.Copy), f"half{n}")
            for n in range(0, 4 * FK, 2):
                act.wait_ge(Tq.sem, Tq.at(f"gu{n}"))
                if n >= 4:
                    act.wait_ge(Vq.sem, Vq.at(f"act{(n - 4) // 2}"))
                a(nc.scalar.activation(gsig[n // 2 % 2][:], bank[n % 4][:], ACT.Sigmoid), f"sig{n // 2}")
            for i in range(TT):
                act.wait_ge(Tq.sem, Tq.at(f"down{i}1"))
                if i >= 2:
                    act.wait_ge(saved[i % 2], 16 * (i // 2))
                a(nc.scalar.activation(rows[i % 2][:, HALF:D], bank[2 * (i % 2) + 1][:], ACT.Copy), f"sh{i}")

        @block.vector
        def _(dve):
            def v(ins, name=None):
                ins.then_inc(Vq.sem, 1)
                Vq.step(name)
                dve.wait_ge(Vq.sem, Vq.here())
            tt, ts, stt, tr = (nc.vector.tensor_tensor, nc.vector.tensor_scalar, nc.vector.scalar_tensor_tensor,
                               nc.vector.tensor_reduce)

            def act_(n):
                fk, h = divmod(n, 2)
                dve.wait_ge(Sq.sem, Sq.at(f"sig{n}"))
                v(tt(gsig[n % 2][:], gsig[n % 2][:], bank[(2 * n) % 4][:], ALU.mult))
                dve.wait_ge(Tq.sem, Tq.at(f"gu{2 * n + 1}"))
                v(tt(actT[:, fk, h * HALF:(h + 1) * HALF], gsig[n % 2][:], bank[(2 * n + 1) % 4][:], ALU.mult), f"act{n}")
            dve.wait_ge(Pq.sem, Pq.at("iotas"))
            for a_, b_ in ((io_f, io_i), (blk_f, blk_i), (io_pf, io_p), (tok_f, tok_i), (pad_f, pad_i)):
                v(nc.vector.tensor_copy(a_[:], b_[:]))

            def over(ap, shape):
                return ap.to_broadcast(shape)
            F3 = [P, TT, NE]
            dve.wait_ge(Sq.sem, Sq.at("scores"))
            dve.wait_ge(w_in["b"], 16)
            v(tt(sel[:], sc[:], over(brow[:].rearrange("p (a e) -> p a e", a=1), F3), ALU.add))
            for i in range(TT):
                for g in range(NG):
                    last = nc.vector.max(g8[:, i, g, :], sel[:, i, g * EG:(g + 1) * EG])
            v(last)
            v(tt(gs[:], g8[:, :, :, 0], g8[:, :, :, 1], ALU.add))

            def top_indices(src):
                for i in range(TT):
                    last = nc.vector.max(top8[:, i, :], src[:, i, :])
                v(last)
                for i in range(TT):
                    last = nc.vector.max_index(idx8[:, i, :], top8[:, i, :], src[:, i, :])
                v(last)
                v(nc.vector.tensor_copy(idxf[:], idx8[:]))
            top_indices(gs)
            G3 = [P, TT, NG]
            iog = io_f[:, 0:NG].rearrange("p (a e) -> p a e", a=1)
            for j in range(TOPG):
                dst = gmask if j == 0 else tmp
                d_ = dst[:, :, 0:NG]
                v(tt(d_, over(iog, G3), over(idxf[:, :, j:j + 1], G3), ALU.is_equal))
                if j:
                    v(tt(gmask[:], gmask[:], d_, ALU.add))
            v(ts(tmp[:, :, 0:NG], gmask[:], -NEG_BIG, NEG_BIG, ALU.mult, ALU.add))
            for i in range(TT):
                gview = lambda x: x.rearrange("p (g e) -> p g e", g=NG)
                gb = lambda x: x.rearrange("p (g a) -> p g a", a=1).to_broadcast([P, NG, EG])
                v(tt(gview(sel[:, i, :]), gview(sel[:, i, :]), gb(gmask[:, i, :]), ALU.mult))
                v(tt(gview(sel[:, i, :]), gview(sel[:, i, :]), gb(tmp[:, i, 0:NG]), ALU.add))
            top_indices(sel)
            io3 = io_f[:].rearrange("p (a e) -> p a e", a=1)
            for j in range(TOPK):
                v(tt(oh[j][:], over(io3, F3), over(idxf[:, :, j:j + 1], F3), ALU.is_equal))
                v(tt(tmp[:], oh[j][:], sc[:], ALU.mult))
                v(tr(pick[:, j, :], tmp[:], AX.X, ALU.add))
                if j:
                    v(tt(M[:], M[:], oh[j][:], ALU.add))
                    v(tt(wsum[:], wsum[:], pick[:, j, :], ALU.add))
                else:
                    v(nc.vector.tensor_copy(M[:], oh[0][:]))
                    v(nc.vector.tensor_copy(wsum[:], pick[:, 0, :]))
            v(nc.vector.memset(Mrun[:, 0, :], 0.0))
            for i in range(TT):
                v(tt(Mrun[:, i + 1, :], Mrun[:, i, :], M[:, i, :], ALU.add), "Mrun" if i == TT - 1 else None)
            v(ts(wsum[:], wsum[:], 1e-20, None, ALU.add))
            v(nc.vector.reciprocal(wsum[:], wsum[:]))
            for j in range(TOPK):
                v(stt(out=entry[j][:, 1, :], in0=pick[:, j, :], scalar=RSCALE, in1=wsum[:], op0=ALU.mult, op1=ALU.mult))
            dve.wait_ge(Tq.sem, Tq.at("ranks"))
            v(nc.vector.tensor_copy(cnt[:], bank[5][:, 0:NE]))
            v(nc.vector.memset(nb_[:], 0.0))
            for m in range(TT):
                v(stt(out=nb_[:], in0=cnt[:], scalar=float(m * P), in1=nb_[:], op0=ALU.is_gt, op1=ALU.add))
            v(nc.vector.tensor_tensor_scan(pend[:], ones[:, 0:NE], nb_[:], 0.0, ALU.mult, ALU.add))
            v(tt(pst[:], pend[:], nb_[:], ALU.subtract))
            v(ts(cnt[:], pst[:], float(P), None, ALU.mult))
            v(tt(rank[:], bank[4][:].rearrange("p (i e) -> p i e", i=TT),
                 over(cnt[:].rearrange("p (a e) -> p a e", a=1), F3), ALU.add))
            for j in range(TOPK):
                v(tt(tmp[:], oh[j][:], rank[:], ALU.mult))
                v(tr(slot[:], tmp[:], AX.X, ALU.add))
                v(nc.vector.tensor_copy(slot_i[:, 1, :], slot[:]))
                v(ts(slot_i[:, 0, :], slot_i[:, 1, :], P - 1, None, ALU.bitwise_and))
                v(ts(slot_i[:, 1, :], slot_i[:, 1, :], P.bit_length() - 1, None, ALU.logical_shift_right))
                v(nc.vector.tensor_copy(slot_f[:], slot_i[:]))
                v(tt(entry[j][:, 0, :], tok_f[:], slot_f[:, 0, :], ALU.subtract))
                if j >= 2:
                    dve.wait_ge(Tq.sem, Tq.at(f"slots{j - 2}"))
                v(tt(place1[j % 2], over(io_pf[:].rearrange("p (a e) -> p a e", a=1), [P, TT, P]),
                     over(slot_f[:, 0, :].rearrange("p (i a) -> p i a", a=1), [P, TT, P]), ALU.is_equal))
                v(tt(block1[j % 2][:, :, 0, :], over(io_pf[:, 0:NB].rearrange("p (a e) -> p a e", a=1), [P, TT, NB]),
                     over(slot_f[:, 1, :].rearrange("p (i a) -> p i a", a=1), [P, TT, NB]), ALU.is_equal), f"hot{j}")
                if j < 4:
                    act_(j)
            v(ts(some[:], nb_[:], 0.0, None, ALU.is_gt))
            v(ts(nb_[:], pend[:], blk_f[:, 0:1], None, ALU.is_le))
            v(tr(be[:, 0:1], nb_[:], AX.X, ALU.add))
            v(ts(be[:, 0:1], be[:, 0:1], float(NE - 1), None, ALU.min))
            v(tt(nb_[:], nb_[:], some[:], ALU.mult))
            v(tr(be[:, 1:2], nb_[:], AX.X, ALU.add))
            v(nc.vector.tensor_copy(buf_i[:], be[:, 1:2]))
            v(ts(buf_i[:], buf_i[:], WBUF - 1, None, ALU.bitwise_and))
            v(nc.vector.tensor_copy(be[:, 1:2], buf_i[:]))
            v(ts(nb_[:], pst[:], blk_f[:, 0:1], None, ALU.is_equal))
            v(tt(nb_[:], nb_[:], some[:], ALU.mult))
            v(tr(be[:, 2:3], nb_[:], AX.X, ALU.add))
            v(nc.vector.tensor_copy(be[:, 3:4], pend[:, NE - 1:NE]), "blocks")
            dve.wait_ge(Tq.sem, Tq.at(f"slots{TOPK - 1}"))
            v(ts(slots[:, 1:NB + 1, 0], bank[6][:, 0:NB], pad_f[:, 0:1], None, ALU.add))
            v(nc.vector.tensor_copy(slots[:, 1:NB + 1, 1].bitcast(F32), bank[6][:, NB:2 * NB]))
            dve.wait_ge(Tq.sem, Tq.at("table"))
            v(nc.vector.tensor_copy(btab[:], bank[7][0:1, :].rearrange("p (x b) -> p x b", x=4)[:, :, 0:NB + 8]))
            for i in range(TT):
                dve.wait_ge(Tq.sem, Tq.at(f"down{i}0"))
                if i >= 2:
                    dve.wait_ge(saved[i % 2], 16 * (i // 2))
                v(nc.vector.tensor_copy(rows[i % 2][:, 0:HALF], bank[2 * (i % 2)][:]), f"sh{i}")
        for x in (Tq, Vq, Sq, Pq):
            x.close()
    mid.close()
    front.close()
    if stop == "route":
        return

    GU = 2 * FD
    fin = ExitStack()
    x1 = at_ctx(fin, "fi_x1", [P, TT, D])
    gfin = at_ctx(fin, "fi_gfin", [P, D])
    x1_in, g_in = sem("fi_x1_in"), sem("fi_g_in")
    with ExitStack() as s:
        wgu = at_ctx(s, "ex_wgu", [P, WBUF, DK, GU])
        wd = at_ctx(s, "ex_wd", [P, WBUF, FK, D])
        xb = [at_ctx(s, f"ex_x{b}", [P, D]) for b in range(4)]
        xbT = [at_ctx(s, f"ex_xT{b}", [P, DK, P]) for b in range(2)]
        sig = at_ctx(s, "ex_sig", [P, FD])
        hid = at_ctx(s, "ex_hid", [P, FD])
        hidT = at_ctx(s, "ex_hidT", [P, FK, P])
        y = [at_ctx(s, f"ex_y{b}", [P, D]) for b in range(2)]
        tok_in = [at_ctx(s, f"ex_tok_in{b}", [P, 1], I32) for b in range(4)]
        tok_out = at_ctx(s, "ex_tok_out", [P, 1], I32)
        wt = [at_ctx(s, f"ex_wt{b}", [P, 1]) for b in range(4)]
        w_in = [sem(f"ex_w{b}_in") for b in range(4)]
        x_in = [sem(f"ex_x{b}_in") for b in range(4)]
        added = sem("ex_added")
        passed = sem("ex_passed")
        init = sem("ex_init")
        first_rows = sem("ex_first_rows")
        in_read, out_read = sem("ex_in_read"), sem("ex_out_read")
        gu_done = sem("ex_gu_done")
        rows_done = sem("ex_rows_done")
        hidT_done = sem("ex_hidT_done")
        down_done = sem("ex_down_done")
        silu_done = sem("ex_silu_done")
        sig_done = sem("ex_sig_done")
        hid_done = sem("ex_hid_done")
        xbT_s, xbT_v = sem("ex_xbT_scalar"), sem("ex_xbT_vector")
        hidT_s = sem("ex_hidT_copied")
        y_s, y_v = sem("ex_y_scalar"), sem("ex_y_vector")
        add_done = sem("ex_add_done")
        START = ((rows_done, 3), (down_done, 6), (hid_done, 1), (hidT_s, 1), (y_s, 1), (y_v, 1), (add_done, 2))
        block = s.enter_context(nc.Block())
        ROUNDS = NB // 4 + 1

        def n_blocks(eng):
            return eng.value_load(btab[0:1, 3, 0:1], min_val=1, max_val=NB)

        def table(eng, row, column, top_):
            return eng.value_load(btab[0:1, column, bass.ds(row, 1)], min_val=0, max_val=top_)

        @block.sync
        def _(sp):
            n = n_blocks(sp)
            with sp.Fori(0, ROUNDS) as i:
                with sp.If(i * 4 <= n):
                    for q in range(4):
                        b = i * 4 + q
                        with sp.If(b < n):
                            e = table(sp, b + 1, 0, NE - 1)
                            slot = table(sp, b + 1, 1, WBUF - 1)
                            new = table(sp, b + 1, 2, 1)
                            sp.wait_ge(down_done, b * 2 + 2)
                            for x, nm in enumerate(("w_exp_gate", "w_exp_up")):
                                sp.dma_start(wgu[:, bass.ds(slot, 1), :, x * FD:(x + 1) * FD].rearrange("p b k n -> p (b k) n"),
                                             f[nm][0][bass.ds(e, 1)].rearrange("e (p k) n -> (e p) k n", k=DK),
                                             cond=new > 0).then_inc(w_in[q], 16)
                            sp.dma_start(wd[:, bass.ds(slot, 1), :, :].rearrange("p b k n -> p (b k n)"),
                                         f["w_exp_down"][0][bass.ds(e, 1)].rearrange("e (p k) n -> (e p) (k n)", k=FK),
                                         cond=new > 0).then_inc(w_in[q], 16)

            sp.dma_start(gfin[:], f["g_final"].rearrange("(a d) -> a d", a=1).to_broadcast([P, D])).then_inc(g_in, 16)
            sp.dma_start(x1[:], x1d.rearrange("(i p) d -> p i d", p=P)).then_inc(x1_in, 16)

        @block.gpsimd
        def _(pool):
            pl = nc.gpsimd
            for x, k in START:
                pl.sem_inc(x, k)
            for b in range(3):
                pl.tensor_copy(tok_in[b][:], slots[:, b + 1, 0:1]).then_inc(init, 1)
            for b in (-1, 0):
                pl.tensor_copy(wt[b % 4][:], slots[:, b + 1, 1:2].bitcast(F32)).then_inc(init, 1)
            pl.memset(hidT[:], 0.0).then_inc(init, 1)
            pool.wait_ge(init, 6)
            for b in range(3):
                pool.indirect_dma_start(xb[b][:], None, hpad, bass.IndirectOffsetOnAxis(ap=tok_in[b][:], axis=0))\
                    .then_inc(x_in[b], 16)
            n = n_blocks(pool)

            def column(b):
                return slots[:, bass.ds(b, 1), :].rearrange("p a c -> p (a c)")

            with pool.Fori(0, ROUNDS) as i:
                with pool.If(i * 4 <= n):
                    for q in range(4):
                        b, q3 = i * 4 + q, (q + 3) % 4
                        with pool.If(b < n):
                            pool.wait_ge(rows_done, b + 2)
                            pool.sem_inc(passed, 1)
                            pl.tensor_copy(tok_in[q3][:], column(b + 4)[:, 0:1]).then_inc(in_read, 1)
                            pl.tensor_copy(wt[(q + 1) % 4][:], column(b + 2)[:, 1:2].bitcast(F32)).then_inc(in_read, 1)
                            pool.wait_ge(in_read, b * 2 + 2)
                            pool.sem_inc(passed, 1)
                            pool.indirect_dma_start(xb[q3][:], None, hpad,
                                                    bass.IndirectOffsetOnAxis(ap=tok_in[q3][:], axis=0)).then_inc(x_in[q3], 16)
                        with pool.If(b <= n):
                            pl.tensor_copy(tok_out[:], column(b)[:, 0:1]).then_inc(out_read, 1)
                            pool.wait_ge(out_read, b + 1)
                            pool.wait_ge(y_s, b + 2)
                            pool.wait_ge(y_v, b + 2)
                            pool.sem_inc(passed, 1)
                            pool.indirect_dma_start(accd, bass.IndirectOffsetOnAxis(ap=tok_out[:], axis=0), y[q3 % 2][:],
                                                    None, compute_op=ALU.add).then_inc(added, 16)
                            pool.wait_ge(added, b * 16 + 16)
                            pool.sem_inc(add_done, 1)

        @block.tensor
        def _(pe):
            def rows_T(q):
                for k in range(DK):
                    last = nc.tensor.transpose(bank[k // 4][:, (k % 4) * P:(k % 4 + 1) * P], xb[q][:, k::DK], ident[:])
                return last
            n = n_blocks(pe)
            pe.wait_ge(x_in[0], 16)
            rows_T(0).then_inc(first_rows, 1)
            with pe.Fori(0, ROUNDS) as i:
                with pe.If(i * 4 <= n):
                    for q in range(4):
                        b, q3 = i * 4 + q, (q + 1) % 4
                        with pe.If(b < n):
                            slot = table(pe, b + 1, 1, WBUF - 1)
                            pe.wait_ge(w_in[q], i * 48 + 48)
                            pe.wait_ge(xbT_v, b + 1)
                            pe.wait_ge(xbT_s, b + 1)
                            for k in range(DK):
                                last = nc.tensor.matmul(bank[2 + q % 2][:], xbT[q % 2][:, k, :],
                                                        wgu[:, bass.ds(slot, 1), k, :].rearrange("p b n -> p (b n)"),
                                                        start=(k == 0), stop=(k == DK - 1))
                            last.then_inc(gu_done, 1)
                            pe.wait_ge(x_in[q3], i * 16 + (16 if q < 3 else 32))
                            rows_T(q3).then_inc(rows_done, 1)
                        with pe.If(b <= n):
                            slot = table(pe, b, 1, WBUF - 1)
                            pe.wait_ge(hidT_s, b + 1)
                            for h in range(2):
                                pe.wait_ge(y_v if h else y_s, b + 1)
                                for k in range(FK):
                                    last = nc.tensor.matmul(bank[6 + h][:], hidT[:, k, :],
                                                            wd[:, bass.ds(slot, 1), k, h * HALF:(h + 1) * HALF]
                                                            .rearrange("p b n -> p (b n)"),
                                                            start=(k == 0), stop=(k == FK - 1))
                                last.then_inc(down_done, 1)
                        with pe.If(b < n):
                            pe.wait_ge(hid_done, b + 2)
                            for k in range(FK):
                                last = nc.tensor.transpose(bank[4][:, k * P:(k + 1) * P], hid[:, k::FK], ident[:])
                            last.then_inc(hidT_done, 1)

        @block.scalar
        def _(act):
            n = n_blocks(act)
            act.wait_ge(first_rows, 1)
            nc.scalar.activation(xbT[0][:, 4:8, :].rearrange("p k t -> p (k t)"), bank[1][:], ACT.Copy).then_inc(xbT_s, 1)
            nc.scalar.preload_act_table(ACT.Sigmoid)
            with act.Fori(0, ROUNDS) as i:
                with act.If(i * 4 <= n):
                    for q in range(4):
                        b, q3, q1 = i * 4 + q, (q + 1) % 4, (q + 3) % 4
                        with act.If(b < n):
                            act.wait_ge(gu_done, b + 1)
                            act.wait_ge(hid_done, b + 1)
                            nc.scalar.activation(sig[:], bank[2 + q % 2][:, 0:FD], ACT.Sigmoid).then_inc(sig_done, 1)
                            act.wait_ge(rows_done, b + 4)
                            nc.scalar.activation(xbT[q3 % 2][:, 4:8, :].rearrange("p k t -> p (k t)"), bank[1][:],
                                                 ACT.Copy).then_inc(xbT_s, 1)
                        with act.If(b <= n):
                            act.wait_ge(down_done, b * 2 + 7)
                            act.wait_ge(add_done, b + 1)
                            nc.scalar.activation(y[q1 % 2][:, 0:HALF], bank[6][:], ACT.Copy, scale=wt[q1][:]).then_inc(y_s, 1)
                        with act.If(b < n):
                            act.wait_ge(hidT_done, b + 1)
                            nc.scalar.activation(hidT[:].rearrange("p k t -> p (k t)"), bank[4][:, 0:FK * P],
                                                 ACT.Copy).then_inc(hidT_s, 1)

        @block.vector
        def _(dve):
            n = n_blocks(dve)
            dve.wait_ge(first_rows, 1)
            nc.vector.tensor_copy(xbT[0][:, 0:4, :].rearrange("p k t -> p (k t)"), bank[0][:]).then_inc(xbT_v, 1)
            with dve.Fori(0, ROUNDS) as i:
                with dve.If(i * 4 <= n):
                    for q in range(4):
                        b, q3, q1 = i * 4 + q, (q + 1) % 4, (q + 3) % 4
                        with dve.If(b < n):
                            dve.wait_ge(sig_done, b + 1)
                            nc.vector.tensor_tensor(sig[:], sig[:], bank[2 + q % 2][:, 0:FD], ALU.mult).then_inc(silu_done, 1)
                            dve.wait_ge(silu_done, b + 1)
                            nc.vector.tensor_tensor(hid[:], sig[:], bank[2 + q % 2][:, FD:GU], ALU.mult).then_inc(hid_done, 1)
                            dve.wait_ge(rows_done, b + 4)
                            nc.vector.tensor_copy(xbT[q3 % 2][:, 0:4, :].rearrange("p k t -> p (k t)"), bank[0][:])\
                                .then_inc(xbT_v, 1)
                        with dve.If(b <= n):
                            dve.wait_ge(down_done, b * 2 + 8)
                            dve.wait_ge(add_done, b + 1)
                            nc.vector.tensor_scalar(y[q1 % 2][:, HALF:D], bank[7][:], wt[q1][:], None, ALU.mult).then_inc(y_v, 1)
    if stop == "experts":
        return

    with ExitStack() as s:
        acc = at_ctx(s, "fi_acc", [P, TT, D])
        gate = at_ctx(s, "fi_gate", [P, D])
        scr = at_ctx(s, "fi_scr", [P, D])
        ss = at_ctx(s, "fi_ss", [P, TT])
        Tf, Vf, Sf, Pf = phase("final")
        a_in = [sem(f"fi_acc{b}_in") for b in range(TT)]
        saved = sem("fi_saved")
        block = s.enter_context(nc.Block())

        @block.sync
        def _(sp):
            for i in range(TT):
                sp.dma_start(acc[:, i, :], accd[i * P:(i + 1) * P, :]).then_inc(a_in[i], 16)
            for i in range(TT):
                sp.wait_ge(Pf.sem, Pf.at(f"out{i}"))
                sp.dma_start(out[0, i * P:(i + 1) * P, :], acc[:, i, :]).then_inc(saved, 16)
            sp.wait_ge(saved, 16 * TT)

        @block.tensor
        def _(pe):
            for j in range(DK):
                last = nc.tensor.matmul(bank[j // 4][:, (j % 4) * P:(j % 4 + 1) * P],
                                        mod[:, GT_F, j:j + 1].to_broadcast([P, P]), ident[:], start=True, stop=True)
            last.then_inc(Tf.sem, 1)
            Tf.step("gate")

        @block.gpsimd
        def _(pool):
            pool.wait_ge(g_in, 16)
            for i in range(TT):
                pool.wait_ge(Sf.sem, Sf.at(f"scaled{i}"))
                nc.gpsimd.tensor_tensor(acc[:, i, :], acc[:, i, :], gfin[:], ALU.mult).then_inc(Pf.sem, 1)
                Pf.step(f"out{i}")

        @block.scalar
        def _(act):
            def a(ins, name=None):
                ins.then_inc(Sf.sem, 1)
                Sf.step(name)
                act.wait_ge(Sf.sem, Sf.here())

            def scale(i):
                act.wait_ge(Vf.sem, Vf.at(f"inv{i}"))
                a(nc.scalar.activation(acc[:, i, :], acc[:, i, :], ACT.Copy, scale=ss[:, i:i + 1]), f"scaled{i}")

            nc.scalar.preload_act_table(ACT.Sqrt)
            for i in range(TT):
                act.wait_ge(Vf.sem, Vf.at(f"x{i}"))
                a(nc.scalar.activation(scr[:], acc[:, i, :], ACT.Square, accum_out=ss[:, i:i + 1]))
                a(nc.scalar.activation(ss[:, i:i + 1], ss[:, i:i + 1], ACT.Sqrt, scale=1.0 / D, bias=eps_rms[:]), f"rms{i}")
                if i:
                    scale(i - 1)
            scale(TT - 1)

        @block.vector
        def _(dve):
            def v(ins, name=None):
                ins.then_inc(Vf.sem, 1)
                Vf.step(name)
                dve.wait_ge(Vf.sem, Vf.here())

            def inv(i):
                dve.wait_ge(Sf.sem, Sf.at(f"rms{i}"))
                v(nc.vector.reciprocal(ss[:, i:i + 1], ss[:, i:i + 1]), f"inv{i}")
            dve.wait_ge(Tf.sem, Tf.at("gate"))
            for half in range(2):
                v(nc.vector.tensor_copy(gate[:].rearrange("t (p j) -> t j p", j=DK)[:, 4 * half:4 * half + 4, :],
                                        bank[half][:].rearrange("t (j p) -> t j p", j=4)))
            dve.wait_ge(x1_in, 16)
            for i in range(TT):
                dve.wait_ge(a_in[i], 16)
                v(nc.vector.tensor_tensor(acc[:, i, :], acc[:, i, :], gate[:], ALU.mult))
                v(nc.vector.tensor_tensor(acc[:, i, :], acc[:, i, :], x1[:, i, :], ALU.add), f"x{i}")
                if i:
                    inv(i - 1)
            inv(TT - 1)
        for x in (Tf, Vf, Sf, Pf):
            x.close()
    fin.close()
    done()


_SKIPPED = ("w_vres", "mu_vres", "rw_v0", "rw_v2")


def kernel(**inputs):
    import numpy as np
    import concourse.bacc as bacc
    from concourse.bass_utils import run_bass_kernel_spmd

    arrays = {f"in_{k}": np.ascontiguousarray(v) for k, v in inputs.items() if k not in _SKIPPED}
    shape = inputs["x"].shape
    known = {}
    for _ in range(2):
        nc = bacc.Bacc("TRN2", target_bir_lowering=False, num_devices=1)
        ins = {k[3:]: nc.dram_tensor(k, a.shape, mybir.dt.from_np(a.dtype), kind="ExternalInput").ap()
               for k, a in arrays.items()}
        out = nc.dram_tensor("out", shape, F32, kind="ExternalOutput").ap()
        build(nc, ins, out, known)
    r = run_bass_kernel_spmd(nc, [arrays], core_ids=[0])
    return r.results[0]["out"]
```
